# Optimizing a Trainium2 kernel written in Bass

```python
import jax, jax.numpy as jnp
from jax import lax
import numpy as np

D_MODEL = 2048
BATCH = 1
SEQ = 256
DEPTH = 1

RMS_EPS = 1e-6
ATTN_HEADS = 16
ATTN_HEAD_DIM = 128
Q_LORA = 512
KV_LORA = 256
IDX_HEADS = 16
IDX_DIM = 64
INDEX_TOPK = 256
Q_BLOCK = 128
SSM_EXPAND = 2
SSM_INNER = SSM_EXPAND * D_MODEL
SSM_HEAD_DIM = 64
SSM_HEADS = SSM_INNER // SSM_HEAD_DIM
SSM_GROUPS = 8
SSM_HEADS_PER_GROUP = SSM_HEADS // SSM_GROUPS
SSM_STATE = 128
SSM_CONV = 4
SSM_CONV_DIM = SSM_INNER + 2 * SSM_GROUPS * SSM_STATE
SSM_CHUNK = 256
PEER_HEADS = 8
PEER_NKEYS = 128
PEER_EXPERTS = PEER_NKEYS * PEER_NKEYS
PEER_KEY_DIM = 128
PEER_TOPK = 16
PEER_BLOCK = 128
IN_WIDTHS = (Q_LORA, KV_LORA, IDX_DIM, IDX_HEADS, SSM_INNER, SSM_CONV_DIM, SSM_HEADS, D_MODEL, D_MODEL)
IN_WIDTH = sum(IN_WIDTHS)
IN_OFFSETS = tuple(int(o) for o in np.cumsum(IN_WIDTHS)[:-1])

kernel_name = "hybrid_dsa_mamba2_peer_block"

def rms_norm(x, g):
    xf = x.astype(jnp.float32)
    y = xf * lax.rsqrt(jnp.mean(xf * xf, axis=-1, keepdims=True) + RMS_EPS)
    return (y * g.astype(jnp.float32)).astype(x.dtype)

def to_blocks(a, blk):
    b, s = a.shape[:2]
    return a.reshape(b, s // blk, blk, *a.shape[2:]).swapaxes(0, 1)

def from_blocks(a):
    nb, b, blk = a.shape[:3]
    return a.swapaxes(0, 1).reshape(b, nb * blk, *a.shape[3:])

def sparse_attention(q, k, v, q_idx, k_idx, w_idx):
    b, s = q.shape[:2]
    k_top = min(INDEX_TOPK, s // 4)
    n_blk = s // Q_BLOCK
    s_pos = jnp.arange(s)
    scale = ATTN_HEAD_DIM ** -0.5
    idx_scale = IDX_DIM ** -0.5

    def block(args):
        t0, qb, qib, wib = args
        t_pos = t0 + jnp.arange(Q_BLOCK)
        logits = jnp.einsum('bqhd,bsd->bqhs', qib, k_idx)
        score = jnp.einsum('bqhs,bqh->bqs', jax.nn.relu(logits), wib).astype(jnp.float32) * idx_scale
        causal = s_pos[None, :] <= t_pos[:, None]
        score = jnp.where(causal[None], score, -jnp.inf)
        _, sel = lax.top_k(score, k_top)
        kg = jax.vmap(lambda kk, ii: kk[ii])(k, sel)
        vg = jax.vmap(lambda vv, ii: vv[ii])(v, sel)
        att = jnp.einsum('bqhd,bqkhd->bqhk', qb, kg).astype(jnp.float32) * scale
        valid = sel <= t_pos[None, :, None]
        att = jnp.where(valid[:, :, None, :], att, -jnp.inf)
        p = jax.nn.softmax(att, axis=-1).astype(vg.dtype)
        return jnp.einsum('bqhk,bqkhd->bqhd', p, vg)

    t0s = jnp.arange(n_blk) * Q_BLOCK
    out = lax.map(block, (t0s, to_blocks(q, Q_BLOCK), to_blocks(q_idx, Q_BLOCK), to_blocks(w_idx, Q_BLOCK)))
    return from_blocks(out)

def ssd_scan(xs, dt, a_neg, bm, cm):
    b, s = xs.shape[:2]
    pad = (-s) % SSM_CHUNK
    n_c = (s + pad) // SSM_CHUNK

    def chunks(a):
        a = jnp.pad(a, [(0, 0), (0, pad)] + [(0, 0)] * (a.ndim - 2))
        return a.reshape(b, n_c, SSM_CHUNK, *a.shape[2:]).swapaxes(0, 1)

    causal = jnp.tril(jnp.ones((SSM_CHUNK, SSM_CHUNK), bool))

    def step(state, inp):
        xc, dtc, bc, cc = inp
        cum = jnp.cumsum(dtc * a_neg, axis=1)
        diff = cum[:, :, None, :] - cum[:, None, :, :]
        decay = jnp.exp(jnp.where(causal[None, :, :, None], diff, -jnp.inf))
        cb = jnp.repeat(jnp.einsum('btgn,bsgn->btsg', cc, bc), SSM_HEADS_PER_GROUP, axis=-1)
        y_intra = jnp.einsum('btsh,bshp->bthp', cb * decay * dtc[:, None, :, :], xc)
        ch = jnp.repeat(cc, SSM_HEADS_PER_GROUP, axis=2)
        bh = jnp.repeat(bc, SSM_HEADS_PER_GROUP, axis=2)
        y_inter = jnp.einsum('bthn,bhpn->bthp', ch, state) * jnp.exp(cum)[..., None]
        w_end = jnp.exp(cum[:, -1:, :] - cum) * dtc
        new_state = state * jnp.exp(cum[:, -1, :])[:, :, None, None] + jnp.einsum('bsh,bshn,bshp->bhpn', w_end, bh, xc)
        return new_state, y_intra + y_inter

    state0 = jnp.zeros((b, SSM_HEADS, SSM_HEAD_DIM, SSM_STATE), jnp.float32)
    _, y = lax.scan(step, state0, (chunks(xs), chunks(dt), chunks(bm), chunks(cm)))
    return y.swapaxes(0, 1).reshape(b, n_c * SSM_CHUNK, SSM_HEADS, SSM_HEAD_DIM)[:, :s]

def mamba2_mixer(z, xbc, dt_raw, conv_w, conv_b, dt_bias, a_log, d_skip, g_ssm):
    b, s = z.shape[:2]
    xbc = lax.conv_general_dilated(xbc, conv_w[:, None, :], window_strides=(1,), padding=[(SSM_CONV - 1, 0)],
                                   dimension_numbers=('NWC', 'WIO', 'NWC'), feature_group_count=SSM_CONV_DIM) + conv_b
    xbc = jax.nn.silu(xbc)
    xs, bm, cm = jnp.split(xbc, [SSM_INNER, SSM_INNER + SSM_GROUPS * SSM_STATE], axis=-1)
    xs = xs.reshape(b, s, SSM_HEADS, SSM_HEAD_DIM).astype(jnp.float32)
    bm = bm.reshape(b, s, SSM_GROUPS, SSM_STATE).astype(jnp.float32)
    cm = cm.reshape(b, s, SSM_GROUPS, SSM_STATE).astype(jnp.float32)
    dt = jax.nn.softplus(dt_raw.astype(jnp.float32) + dt_bias.astype(jnp.float32))
    a_neg = -jnp.exp(a_log.astype(jnp.float32))
    y = ssd_scan(xs, dt, a_neg, bm, cm)
    y = y + d_skip.astype(jnp.float32)[:, None] * xs
    y = y.reshape(b, s, SSM_INNER) * jax.nn.silu(z.astype(jnp.float32))
    yg = y.reshape(b, s, SSM_GROUPS, SSM_INNER // SSM_GROUPS)
    yg = yg * lax.rsqrt(jnp.mean(yg * yg, axis=-1, keepdims=True) + RMS_EPS)
    y = yg.reshape(b, s, SSM_INNER) * g_ssm.astype(jnp.float32)
    return y.astype(z.dtype)

def peer_ffn(h, w_peer_q, peer_keys, peer_u, peer_v):
    b, s, _ = h.shape
    q = (h @ w_peer_q).reshape(b, s, PEER_HEADS, 2, PEER_KEY_DIM)
    sc = jnp.einsum('bshcd,hckd->bshck', q, peer_keys).astype(jnp.float32)
    s1, i1 = lax.top_k(sc[..., 0, :], PEER_TOPK)
    s2, i2 = lax.top_k(sc[..., 1, :], PEER_TOPK)
    cand_s = (s1[..., :, None] + s2[..., None, :]).reshape(b, s, PEER_HEADS, PEER_TOPK * PEER_TOPK)
    cand_i = (i1[..., :, None] * PEER_NKEYS + i2[..., None, :]).reshape(b, s, PEER_HEADS, PEER_TOPK * PEER_TOPK)
    top_s, pos = lax.top_k(cand_s, PEER_TOPK)
    eid = jnp.take_along_axis(cand_i, pos, axis=-1)
    gate = jax.nn.softmax(top_s, axis=-1).astype(h.dtype)

    def block(args):
        hb, eb, gb = args
        u = peer_u[eb]
        act = jax.nn.gelu(jnp.einsum('bthkd,btd->bthk', u, hb), approximate=False)
        vv = peer_v[eb]
        return jnp.einsum('bthk,bthkd->btd', gb * act, vv)

    out = lax.map(block, (to_blocks(h, PEER_BLOCK), to_blocks(eid, PEER_BLOCK), to_blocks(gate, PEER_BLOCK)))
    return from_blocks(out)

def hybrid_layer(x, g_norm1, w_in, g_cq, g_ckv, w_uq, w_ukv, g_qn, g_kn, w_iq, w_o_attn,
                 conv_w, conv_b, dt_bias, a_log, d_skip, g_ssm, w_o_ssm, w_out,
                 g_norm2, w_peer_q, peer_keys, peer_u, peer_v):
    b, s, _ = x.shape
    h = rms_norm(x, g_norm1)
    proj = h @ w_in
    c_q, c_kv, k_idx, w_idx, z, xbc, dt_raw, gate_a, gate_b = jnp.split(proj, IN_OFFSETS, axis=-1)
    cq = rms_norm(c_q, g_cq)
    ckv = rms_norm(c_kv, g_ckv)
    q = rms_norm((cq @ w_uq).reshape(b, s, ATTN_HEADS, ATTN_HEAD_DIM), g_qn)
    kv = (ckv @ w_ukv).reshape(b, s, ATTN_HEADS, 2 * ATTN_HEAD_DIM)
    k = rms_norm(kv[..., :ATTN_HEAD_DIM], g_kn)
    v = kv[..., ATTN_HEAD_DIM:]
    q_idx = (cq @ w_iq).reshape(b, s, IDX_HEADS, IDX_DIM)
    attn = sparse_attention(q, k, v, q_idx, k_idx, w_idx * IDX_HEADS ** -0.5)
    y_a = attn.reshape(b, s, ATTN_HEADS * ATTN_HEAD_DIM) @ w_o_attn
    y_b = mamba2_mixer(z, xbc, dt_raw, conv_w, conv_b, dt_bias, a_log, d_skip, g_ssm) @ w_o_ssm
    mixed = jax.nn.sigmoid(gate_a) * y_a + jax.nn.sigmoid(gate_b) * y_b
    x = x + mixed @ w_out
    x = x + peer_ffn(rms_norm(x, g_norm2), w_peer_q, peer_keys, peer_u, peer_v)
    return x

def setup_inputs(seed: int = 0) -> dict:
    key = jax.random.key(seed)
    ks = jax.random.split(key, 26)
    L = DEPTH
    f32 = jnp.float32

    def nrm(k, shape, fan_in):
        return jax.random.normal(k, shape, f32) * (fan_in ** -0.5)

    def gain(k, n):
        return 1.0 + 0.02 * jax.random.normal(k, (L, n), f32)

    dt0 = jnp.exp(jax.random.uniform(ks[13], (L, SSM_HEADS), f32, minval=float(np.log(1e-3)), maxval=float(np.log(1e-1))))
    return {
        "x": jax.random.normal(ks[0], (BATCH, SEQ, D_MODEL), f32),
        "g_norm1": gain(ks[1], D_MODEL),
        "w_in": nrm(ks[2], (L, D_MODEL, IN_WIDTH), D_MODEL),
        "g_cq": gain(ks[3], Q_LORA),
        "g_ckv": gain(ks[4], KV_LORA),
        "w_uq": nrm(ks[5], (L, Q_LORA, ATTN_HEADS * ATTN_HEAD_DIM), Q_LORA),
        "w_ukv": nrm(ks[6], (L, KV_LORA, ATTN_HEADS * 2 * ATTN_HEAD_DIM), KV_LORA),
        "g_qn": gain(ks[7], ATTN_HEAD_DIM),
        "g_kn": gain(ks[8], ATTN_HEAD_DIM),
        "w_iq": nrm(ks[9], (L, Q_LORA, IDX_HEADS * IDX_DIM), Q_LORA),
        "w_o_attn": nrm(ks[10], (L, ATTN_HEADS * ATTN_HEAD_DIM, D_MODEL), ATTN_HEADS * ATTN_HEAD_DIM),
        "conv_w": nrm(ks[11], (L, SSM_CONV, SSM_CONV_DIM), SSM_CONV),
        "conv_b": 0.02 * jax.random.normal(ks[12], (L, SSM_CONV_DIM), f32),
        "dt_bias": dt0 + jnp.log(-jnp.expm1(-dt0)),
        "a_log": jnp.log(jax.random.uniform(ks[14], (L, SSM_HEADS), f32, minval=1.0, maxval=16.0)),
        "d_skip": 1.0 + 0.1 * jax.random.normal(ks[15], (L, SSM_HEADS), f32),
        "g_ssm": gain(ks[16], SSM_INNER),
        "w_o_ssm": nrm(ks[17], (L, SSM_INNER, D_MODEL), SSM_INNER),
        "w_out": nrm(ks[18], (L, D_MODEL, D_MODEL), D_MODEL),
        "g_norm2": gain(ks[19], D_MODEL),
        "w_peer_q": nrm(ks[20], (L, D_MODEL, PEER_HEADS * 2 * PEER_KEY_DIM), D_MODEL),
        "peer_keys": nrm(ks[21], (L, PEER_HEADS, 2, PEER_NKEYS, PEER_KEY_DIM), PEER_KEY_DIM),
        "peer_u": nrm(ks[22], (L, PEER_EXPERTS, D_MODEL), D_MODEL),
        "peer_v": nrm(ks[23], (L, PEER_EXPERTS, D_MODEL), PEER_HEADS),
    }

def reference(x, g_norm1, w_in, g_cq, g_ckv, w_uq, w_ukv, g_qn, g_kn, w_iq, w_o_attn,
              conv_w, conv_b, dt_bias, a_log, d_skip, g_ssm, w_o_ssm, w_out,
              g_norm2, w_peer_q, peer_keys, peer_u, peer_v):
    for layer in range(DEPTH):
        x = hybrid_layer(x, g_norm1[layer], w_in[layer], g_cq[layer], g_ckv[layer], w_uq[layer], w_ukv[layer],
                         g_qn[layer], g_kn[layer], w_iq[layer], w_o_attn[layer],
                         conv_w[layer], conv_b[layer], dt_bias[layer], a_log[layer], d_skip[layer], g_ssm[layer],
                         w_o_ssm[layer], w_out[layer], g_norm2[layer], w_peer_q[layer], peer_keys[layer],
                         peer_u[layer], peer_v[layer])
    return x


_drawn_inputs = setup_inputs


def setup_inputs(seed=0):
    import zlib

    import numpy as np

    out = dict(_drawn_inputs(seed))
    spreads = {}
    factors = {'g_cq': 3.142,
     'g_ckv': 5.605,
     'g_qn': 6.281,
     'g_kn': 7.519,
     'g_ssm': 16.726,
     'conv_b': 3.958,
     'g_norm2': 7.468}
    for name, (base, spread) in spreads.items():
        noise = np.random.default_rng([zlib.crc32(name.encode()), seed]).standard_normal(out[name].shape)
        drawn = base * np.exp(spread * noise) if base else spread * noise
        out[name] = __import__('jax').numpy.asarray(drawn.astype(out[name].dtype))
    for name, factor in factors.items():
        out[name] = (out[name] * factor).astype(out[name].dtype)
    return out
```

```python
from contextlib import ExitStack

import concourse.bass as bass
from concourse import mybir

ALU = mybir.AluOpType
ACT = mybir.ActivationFunctionType
AX = mybir.AxisListType
F32 = mybir.dt.float32
F32R = mybir.dt.float32r
I32 = mybir.dt.int32
U32 = mybir.dt.uint32

P = 128
BANK = 512
PIECE_KC = 2
RING = 4
AHEAD = RING - 1
GATHERS = 8
NEG = -1.0e30
FAR = 3.0e38
TAKEN = -3.4e38
EPS = 1e-6
RSQRT_MAGIC = float(0x5F3759DF)


class Steps:

    def __init__(self, eng, sem):
        self.eng, self.sem, self.n, self.offset = eng, sem, 0, 0

    def mark(self, instruction):
        instruction.then_inc(self.sem, 1)
        self.n += 1
        return self.n

    def wait(self, n=None):
        self.eng.wait_ge(self.sem, self.offset + (self.n if n is None else n))

    def wait_apart(self, passed):
        self.wait()
        self.eng.sem_inc(passed, 1)

    def enter(self, index, per_trip):
        self.start, self.per = self.n, per_trip
        self.offset = index * per_trip

    def leave(self, trips):
        assert self.n - self.start == self.per, (self.n - self.start, self.per)
        self.n, self.offset = self.start + self.per * trips, 0


def hybrid_block(nc, x, g_norm1, w_in, g_cq, g_ckv, w_uq, w_ukv, g_qn, g_kn, w_iq, w_o_attn,
                 conv_w, conv_b, dt_bias, a_log, d_skip, g_ssm, w_o_ssm, w_out,
                 g_norm2, w_peer_q, peer_keys, peer_u, peer_v, out):
    T, D = x.shape[1], x.shape[2]
    NT = T // P
    KC = D // P
    QL, KVL = g_cq.shape[1], g_ckv.shape[1]
    HD = g_qn.shape[1]
    HEADS = w_uq.shape[2] // HD
    IDXH = 16
    IDXD = w_iq.shape[2] // IDXH
    TOPK = T // 4
    SH = dt_bias.shape[1]
    INNER = g_ssm.shape[1]
    SG = 8
    GH = SH // SG
    SHD = INNER // SH
    CONVD = conv_w.shape[2]
    CC = CONVD // P
    XC = INNER // P
    TAPS = conv_w.shape[1]
    PH = peer_keys.shape[1]
    NK = peer_keys.shape[3]
    PK = 16
    assert NT == 2 and D == 4 * BANK and HD == P and NK == P and SG * BANK == INNER

    c_cq = 0
    c_ckv = c_cq + QL
    c_kidx = c_ckv + KVL
    c_widx = c_kidx + IDXD
    c_z = c_widx + IDXH
    c_xbc = c_z + INNER
    c_bc = c_xbc + INNER
    c_dt = c_xbc + CONVD
    c_gate = c_dt + SH

    KP = KC // PIECE_KC
    n_first = 0
    n_idx = n_first + 3 * KP
    n_attn = n_idx + 4
    J = 4
    J_P = 2 + 2 + KP
    n_ya = n_attn + J * J_P
    n_ssm = n_ya + 4 * KP
    G_P = 4 * KP
    n_wout = n_ssm + SG * G_P
    n_pq = n_wout + 4 * KP
    n_all = n_pq + 4 * KP
    assert all(n % RING == 0 for n in (n_idx, n_attn, J_P, n_ya, n_ssm, G_P, n_wout, n_pq, n_all))

    top = [(nc.sbuf_base + 63) // 64 * 64]
    most = [0]

    def sb(name, shape, dtype=F32):
        size = 4
        for s in shape[1:]:
            size *= s
        t = nc.alloc_sbuf_tensor_at(name, shape, dtype, offset=top[0])
        top[0] += (size + 31) // 32 * 32
        most[0] = max(most[0], top[0])
        return t

    ident = sb("ident", [P, P])
    ident_r = sb("ident_r", [P, P], F32R)
    cum_rhs0 = sb("cum_rhs0", [P, 3, P], F32R)
    cum_rhs1 = sb("cum_rhs1", [P, 2, P], F32R)
    future_r = sb("future_r", [P, P], F32R)
    tri = sb("tri", [P, P])
    ones = sb("ones", [P, P])
    iota16 = sb("iota16", [P, PK])
    iota_i = sb("iota_i", [P, PK], I32)
    columns = sb("columns", [P, 296])
    steps_bc = sb("steps_bc", [P, 3, SH])
    rq_v = sb("rq_v", [P, 16])
    rq_i = sb("rq_i", [P, 16], I32)
    rq_a = sb("rq_a", [P, 16])
    ss = sb("ss", [P, 16])
    rstd = sb("rstd", [P, 16])
    per_head = sb("per_head", [P, 5, SH])
    da_split = sb("da_split", [P, 4, SH], F32R)
    r_act = top[0]
    act_hi = sb("act_hi", [P, KC, T], F32R)
    act_lo = sb("act_lo", [P, KC, T], F32R)
    w_raw = sb("w_raw", [P, RING, PIECE_KC, BANK])
    w_hi = sb("w_hi", [P, RING, PIECE_KC, BANK], F32R)
    w_lo = sb("w_lo", [P, RING, PIECE_KC, BANK], F32R)
    conv_g = sb("conv_g", [P, TAPS + 1, 4])
    r_bc = top[0]
    bc_t = sb("bc_t", [P, 2 * SG, T])
    r_after_bc = top[0]

    attn_hi = sb("attn_hi", [P, HEADS, T], F32R)
    attn_lo = sb("attn_lo", [P, HEADS, T], F32R)
    r_after_attn = top[0]
    cqt_hi = sb("cqt_hi", [P, QL // P, T], F32R)
    cqt_lo = sb("cqt_lo", [P, QL // P, T], F32R)
    ckvt_hi = sb("ckvt_hi", [P, KVL // P, T], F32R)
    ckvt_lo = sb("ckvt_lo", [P, KVL // P, T], F32R)
    r_qi = top[0]
    qi_t = sb("qi_t", [P, IDXH * IDXD // P, T])
    r_after_qi = top[0]
    ki_t = sb("ki_t", [P, T])
    score = sb("score", [P, NT, T])
    relu = sb("relu", [P, 2, NT, T])
    causal = sb("causal", [P, NT, T])
    keep_c = sb("keep_c", [P, 3 * P])
    keep = sb("keep", [P, 3 * P])
    m8 = sb("m8", [P, 8])
    conv_acc = sb("conv_acc", [P, 4, T])
    sq = sb("sq", [P, 8, HD])
    prob = sb("prob", [P, 4, 3 * P])
    row_max = sb("row_max", [P, 4, NT])
    row_sum = sb("row_sum", [P, 4, NT])
    row_inv = sb("row_inv", [P, 4, NT])
    widx = sb("widx", [P, NT, IDXH])
    r_attn_end = top[0]
    top[0] = r_qi
    q_raw = sb("q_raw", [P, NT, 4, HD])
    prob_t = sb("prob_t", [P, 2, 3 * P])
    assert top[0] <= r_after_qi
    top[0] = r_attn_end
    kv_raw = sb("kv_raw", [P, NT, 4, 2 * HD])
    q_t = sb("q_t", [P, 4, T])
    k_t = sb("k_t", [P, 4, T])

    top[0] = r_after_bc
    x_sb = sb("x_sb", [P, NT, D])
    x_junk = sb("x_junk", [P, D])
    rows = sb("rows", [P, 3, P])
    cqn = sb("cqn", [P, NT, QL])
    assert top[0] <= r_after_attn
    top[0] = r_attn_end
    ckvn = sb("ckvn", [P, NT, KVL])
    kidx2 = sb("kidx2", [P, NT, 2, IDXD])
    sp = sb("sp", [P, 8, NT * SH])

    top[0] = r_after_bc
    gates = sb("gates", [P, NT, 2 * D])
    ya = sb("ya", [P, NT, D])
    yb = sb("yb", [P, NT, D])
    r_after_y = top[0]
    bc_g = sb("bc_g", [P, 2, T])
    per_head_g = sb("per_head_g", [P, 5, GH])
    da_g = sb("da_g", [P, 4, GH], F32R)
    gain_g = sb("gain_g", [P, 4])
    mix_t = sb("mix_t", [P, GH, 3 * P])
    x_ch = sb("x_ch", [P, 4, T])
    x_tok = sb("x_tok", [P, NT, BANK])
    top[0] -= 2 * 4 * 4 * T
    y_skip = sb("y_skip", [P, NT, BANK])
    top[0] += 4 * NT * BANK
    z_act = sb("z_act", [P, NT, BANK])
    yt_hi = sb("yt_hi", [P, 4, T], F32R)
    yt_lo = sb("yt_lo", [P, 4, T], F32R)

    top[0] = r_after_y
    x1 = sb("x1", [P, NT, D])
    keys = sb("keys", [P, 2 * PH, P])
    keys_t = sb("keys_t", [P, 2 * PH, NK])
    assert top[0] <= nc.sbuf_usable_end
    top[0] = r_bc
    gain2 = sb("gain2", [P, D])
    top[0] = r_after_bc
    h2 = sb("h2", [P, NT, D])
    sc = sb("sc", [P, NT, 2 * (PH + 1), NK])
    qp = sb("qp", [P, 2, 4, T])
    sc_u = sb("sc_u", [P, 2, NK])
    top_v = sb("top_v", [P, 2, PK])
    top_i = sb("top_i", [P, 2, PK], U32)
    top_f = sb("top_f", [P, 2, PK])
    cand = sb("cand", [P, PK, PK])
    pair_v = sb("pair_v", [P, PK])
    pair_i = sb("pair_i", [P, PK], U32)
    pair_hl = sb("pair_hl", [P, 2, PK], U32)
    pair_f = sb("pair_f", [P, 2, PK])
    pick = sb("pick", [P, PK, PK])
    part = sb("part", [P, 2, PK])
    eid = sb("eid", [P, NT, PK], U32)
    g_exp = sb("g_exp", [P, PK])
    g_max = sb("g_max", [P, 1])
    g_sum = sb("g_sum", [P, NT])
    g_inv = sb("g_inv", [P, 1])
    gate = sb("gate", [P, NT, PK])
    dots = sb("dots", [P, NT, PK])
    gelu = sb("gelu", [P, NT, PK])
    share = sb("share", [P, NT, PK])
    assert top[0] <= r_after_y
    top[0] = r_act
    slots = sb("slots", [P, GATHERS, D])
    assert top[0] <= r_bc and most[0] <= nc.sbuf_usable_end, most[0]

    with ExitStack() as ctx:
        def sem(name):
            return ctx.enter_context(nc.semaphore(name))

        acc = [ctx.enter_context(nc.psum_tensor(f"acc{i}", [P, 2, BANK], F32)) for i in "AB"]
        A, B = acc
        small = ctx.enter_context(nc.psum_tensor("small", [P, 2, BANK], F32))
        pair_d = ctx.enter_context(nc.psum_tensor("pair_d", [P, 2, BANK], F32))

        raw_landed = [sem(f"raw_landed{i}") for i in range(RING)]
        hi_split = sem("hi_split")
        lo_split = sem("lo_split")
        w_used = sem("w_used")
        acc_free_act = sem("acc_free_act")
        acc_free_dve = sem("acc_free_dve")
        small_full = sem("small_full")
        small_free_act = sem("small_free_act")
        small_free_dve = sem("small_free_dve")
        turned_hi = sem("turned_hi")
        rows_landed = sem("rows_landed")
        x_landed = [sem(f"x_landed{t}") for t in range(NT)]
        steps_landed = sem("steps_landed")
        consts = sem("consts")
        pool_step = sem("pool_step")
        dve_step = sem("dve_step")
        dve_passed = sem("dve_passed")
        pool_passed = sem("pool_passed")
        xn_ready = sem("xn_ready")
        squared = sem("squared")
        sp_in = sem("sp_in")
        sp_exp = sem("sp_exp")
        da_ready = sem("da_ready")
        da_hi = sem("da_hi")
        da_lo = sem("da_lo")
        relu_used = sem("relu_used")
        conv_g_ready = sem("conv_g_ready")
        conv_biased = sem("conv_biased")
        conv_done = sem("conv_done")
        conv_act = sem("conv_act")
        sq_used = sem("sq_used")
        qn_ready = sem("qn_ready")
        masked = sem("masked")
        exped = sem("exped")
        probs = sem("probs")
        group_ready = sem("group_ready")
        cb_full = sem("cb_full")
        mixed_t = sem("mixed_t")
        skip_ready = sem("skip_ready")
        y_full = sem("y_full")
        y_taken = sem("y_taken")
        y_gated = sem("y_gated")
        y_squared = sem("y_squared")
        yn_ready = sem("yn_ready")
        yb_ready = sem("yb_ready")
        mixed = sem("mixed")
        late_landed = [sem(f"late_landed{i}") for i in range(3)]
        x1_squared = sem("x1_squared")
        h2_ready = sem("h2_ready")
        sc_padded = sem("sc_padded")
        unit_sc = sem("unit_sc")
        unit_ids = sem("unit_ids")
        top_ready = sem("top_ready")
        gate_exp = sem("gate_exp")
        gathered = [sem(f"gathered{i}") for i in range(GATHERS)]
        slot_free = sem("slot_free")
        shared = sem("shared")
        gelued = sem("gelued")
        stored = sem("stored")

        U_turn_x = 1
        S0_dve = 1 + 8
        U_first = 9
        U_idx = U_first + 4
        U_cum = U_idx + IDXH
        U_attn = U_cum + 1
        J_U, J_ACT, J_DVE = 14, 4, 10
        sf_act_j, sf_dve_j = IDXH, U_first + 4 + 1
        U_ssm = U_attn + J * J_U
        G_U, G_ACT, G_DVE = 12, 10, 2
        sf_act_g, sf_dve_g = sf_act_j + J * J_ACT, sf_dve_j + J * J_DVE
        U_late = U_ssm + SG * G_U
        sf_act_l, sf_dve_l = sf_act_g + SG * G_ACT, sf_dve_g + SG * G_DVE
        T_j = 8 + 3
        T_g = T_j + J * 2
        T_l = T_g + SG * 2
        af_dve_j, af_act_j = 3, 2
        af_dve_y, af_act_y = af_dve_j + J, af_act_j + 3 * J
        af_dve_g, af_act_g = af_dve_y, af_act_y + 4
        af_dve_l, af_act_l = af_dve_g + 5 * SG, af_act_g + 2 * SG

        N_CONSTS = 7

        class At:

            def __init__(self, k, index=0, per=0):
                self.k, self.index, self.per = k, index, per

            def plus(self, n):
                return At(self.k + n, self.index, self.per)

            def count(self, add=0):
                return self.index * self.per + (self.k + add) if self.per else self.k + add

            def landed(self):
                done = (self.k // RING + 1) * 16
                return self.index * (self.per // RING * 16) + done if self.per else done

        sq_flat = sq[:, :, :].rearrange("p a b -> p (a b)")

        def chan(ps, c):
            return ps[:, c // 2, c % 2 * T:(c % 2 + 1) * T]

        def done(eng, at):
            eng.wait_ge(w_used, at.count(1))

        block = ctx.enter_context(nc.Block())

        @block.sync
        def _(sp):
            def vec(i, row, v):
                n = v.shape[0]
                sp.dma_start(rows[row:row + n, i, :], v).then_inc(rows_landed, 16)

            def by_rows(v):
                return v.rearrange("a (c p) -> (a c) p", p=P)

            for t in range(NT):
                sp.dma_start(x_sb[:, t, :], x[0, t * P:(t + 1) * P, :]).then_inc(x_landed[t], 16)
            taps = conv_w[0].rearrange("k (c p) -> (k c) p", p=P)
            vec(0, 0, taps[0:2 * CC, :])
            vec(1, 0, taps[2 * CC:4 * CC, :])
            at = 0
            for v in (conv_b, g_norm1, g_ssm, g_cq, g_ckv, g_qn, g_kn):
                vec(2, at, by_rows(v))
                at += v.shape[1] // P
            for i, v in enumerate((dt_bias, a_log, d_skip)):
                sp.dma_start(steps_bc[:, i, :], v[0:1, :].broadcast_to([P, SH])).then_inc(steps_landed, 16)

            def piece(n, local, w, row0, col0):
                slot = local % RING
                if not (isinstance(n, int) and n < RING):
                    sp.wait_ge(lo_split, n - RING + 1)
                src = w[0, bass.ds(row0, PIECE_KC * P), bass.ds(col0, BANK)]
                sp.dma_start(w_raw[:, slot], src.rearrange("(k p) n -> p k n", p=P)).then_inc(raw_landed[slot], 16)

            def full_block(n, local, w, col0):
                for j in range(KP):
                    piece(n + j, local + j, w, j * PIECE_KC * P, col0)

            for b, col in enumerate((c_cq, c_ckv, c_dt)):
                full_block(n_first + b * KP, b * KP, w_in, col)
            for b in range(2):
                for j in range(2):
                    piece(n_idx + 2 * b + j, 2 * b + j, w_iq, j * PIECE_KC * P, b * BANK)
            with sp.Fori(0, J) as j:
                n = j * J_P + n_attn
                for k in range(2):
                    piece(n + k, k, w_uq, k * PIECE_KC * P, j * BANK)
                for k in range(2):
                    piece(n + 2 + k, 2 + k, w_ukv, 0, j * (2 * BANK) + k * BANK)
                full_block(n + 4, 4, w_in, j * BANK + c_bc)
            with sp.Fori(0, 2) as d:
                for k in range(2):
                    full_block(d * (2 * KP) + (n_ya + k * KP), k * KP, w_o_attn, d * (2 * BANK) + k * BANK)
            with sp.Fori(0, SG) as g:
                n = g * G_P + n_ssm
                full_block(n, 0, w_in, g * BANK + c_xbc)
                full_block(n + KP, KP, w_in, g * BANK + c_z)
                full_block(n + 2 * KP, 2 * KP, w_in, g * BANK + c_gate)
                for d in range(4):
                    for k in range(2):
                        piece(n + 3 * KP + 2 * d + k, 2 * d + k, w_o_ssm, g * BANK + k * PIECE_KC * P, d * BANK)
            for base, w in ((n_wout, w_out), (n_pq, w_peer_q)):
                with sp.Fori(0, 2) as d:
                    for k in range(2):
                        full_block(d * (2 * KP) + (base + k * KP), k * KP, w, d * (2 * BANK) + k * BANK)
            sp.wait_ge(slot_free, GATHERS + PH * NT * 2 * PK)
            for t in range(NT):
                sp.dma_start(out[0, t * P:(t + 1) * P, :], x1[:, t, :]).then_inc(stored, 16)
            sp.wait_ge(stored, 16 * NT)

        @block.gpsimd
        def _(pool):
            steps = Steps(pool, pool_step)

            def select(t, pattern, base, channel, fill):
                steps.wait()
                return pool.affine_select(out=t, in_=t, pattern=pattern, compare_op=ALU.is_ge, fill=fill,
                                          base=base, channel_multiplier=channel)

            steps.mark(pool.memset(ident[:, :], 0.0))
            steps.mark(pool.memset(tri[:, :], 1.0))
            steps.mark(pool.memset(ones[:, :], 1.0))
            steps.mark(pool.memset(causal[:, :, :], FAR))
            steps.mark(pool.memset(keep_c[:, :], 0.0))
            steps.mark(pool.memset(keep[:, 0:P], 0.0))
            steps.mark(pool.iota(iota_i[:, :], pattern=[[1, PK]], base=0, channel_multiplier=0))
            steps.wait()
            steps.mark(pool.affine_select(out=ident[:, :], in_=ident[:, :], compare_op=ALU.not_equal, fill=1.0,
                                          base=0, pattern=[[-1, P]], channel_multiplier=1))
            steps.mark(select(tri[:, :], [[1, P]], 0, -1, 0.0))
            for t in range(NT):
                steps.mark(select(causal[:, t, :], [[-1, T]], t * P, 1, -FAR))
            steps.mark(select(keep_c[:, 0:P], [[-1, P]], 0, 1, NEG))
            steps.mark(select(keep_c[:, P:3 * P], [[-1, T]], P, 1, NEG))
            steps.mark(select(keep[:, 0:P], [[1, P]], 0, -1, NEG))
            steps.mark(pool.tensor_copy(iota16[:, :], iota_i[:, :]))
            steps.wait()
            pool.tensor_copy(ident_r[:, :], ident[:, :]).then_inc(consts, 1)
            for i, t in enumerate((tri, ones, ones)):
                pool.tensor_copy(cum_rhs0[:, i, :], t[:, :]).then_inc(consts, 1)
            for i in range(2):
                pool.tensor_copy(cum_rhs1[:, i, :], tri[:, :]).then_inc(consts, 1)
            pool.tensor_copy(future_r[:, :], keep[:, 0:P]).then_inc(consts, 1)

            taps = columns[:, 0:(TAPS + 1) * CC].rearrange("p (k c) -> p k c", c=CC)
            pool.wait_ge(small_free_dve, 1)
            with pool.Fori(0, J) as j:
                pool.wait_ge(acc_free_dve, j + af_dve_j)
                pool.tensor_copy(conv_g[:, :, :], taps[:, :, bass.ds(j * 4 + XC, 4)]).then_inc(conv_g_ready, 1)
            pool.wait_ge(steps_landed, 48)
            pool.wait_ge(da_lo, 1)
            pool.wait_ge(small_free_dve, sf_dve_j)
            steps.mark(pool.tensor_copy(per_head[:, 4, :], steps_bc[:, 2, :]))
            steps.wait()
            pool.wait_ge(conv_act, J)
            pool.wait_ge(acc_free_act, af_act_g)
            pool.memset(yb[:, :, :], 0.0).then_inc(yb_ready, 1)
            bc_pairs = bc_t[:, :, :].rearrange("p (k g) t -> p k g t", k=2)
            with pool.Fori(0, SG) as g:
                pool.wait_ge(small_free_dve, g * G_DVE + sf_dve_g)
                pool.tensor_copy(conv_g[:, :, :], taps[:, :, bass.ds(g * 4, 4)]).then_inc(group_ready, 1)
                pool.tensor_copy(bc_g[:, :, :], bc_pairs[:, :, bass.ds(g, 1), :].rearrange("p k g t -> p k (g t)")).then_inc(group_ready, 1)
                pool.tensor_copy(per_head_g[:, :, :], per_head[:, :, bass.ds(g * GH, GH)]).then_inc(group_ready, 1)
                pool.tensor_copy(da_g[:, :, :], da_split[:, :, bass.ds(g * GH, GH)].bitcast(F32)).then_inc(group_ready, 1)
                pool.tensor_copy(gain_g[:, :], columns[:, bass.ds(g * 4 + (5 * CC + KC), 4)]).then_inc(group_ready, 1)
                pool.wait_ge(group_ready, g * 5 + 5)
                pool.wait_ge(small_free_act, g * G_ACT + (sf_act_g + G_ACT))
                for t in range(NT):
                    pool.tensor_tensor(y_skip[:, t, :].rearrange("p (h c) -> p h c", c=SHD),
                                       x_tok[:, t, :].rearrange("p (h c) -> p h c", c=SHD),
                                       per_head_g[:, 4, :].unsqueeze(2).broadcast_to([P, GH, SHD]),
                                       ALU.mult).then_inc(skip_ready, 1)

            pool.wait_ge(small_free_dve, sf_dve_l)
            pool.wait_ge(acc_free_dve, af_dve_l)
            pool.wait_ge(lo_split, n_wout)
            for t in range(NT):
                pool.dma_start(x1[:, t, :], x[0, t * P:(t + 1) * P, :]).then_inc(late_landed[0], 16)
            pool.dma_start(keys[:, :, :], peer_keys[0].rearrange("h c k d -> k (h c) d")).then_inc(late_landed[1], 16)
            pool.dma_start(gain2[:, :], g_norm2[0:1, :].broadcast_to([P, D])).then_inc(late_landed[2], 16)
            pool.wait_ge(small_free_dve, sf_dve_l + 8)
            pool.memset(sc[:, :, 2 * PH:2 * PH + 2, :], 0.0).then_inc(sc_padded, 1)

            with pool.Fori(0, PH) as h:
                for t in range(NT):
                    pool.wait_ge(unit_ids, h * NT + (t + 1))
                    for half, table in enumerate((peer_u[0], peer_v[0])):
                        for k in range(PK):
                            i = (2 * t + half) * PK + k
                            pool.wait_ge(slot_free, h * (2 * NT * PK) + (i + 1))
                            pool.sem_inc(pool_passed, 1)
                            pool.indirect_dma_start(slots[:, i % GATHERS, :], None, table,
                                                    bass.IndirectOffsetOnAxis(ap=eid[:, t, k:k + 1], axis=0)
                                                    ).then_inc(gathered[i % GATHERS], 16)

        @block.scalar
        def _(act):
            def split(at):
                slot = at.k % RING
                act.wait_ge(raw_landed[slot], at.landed())
                if at.per or at.k >= RING:
                    act.wait_ge(w_used, at.count(1 - RING))
                act.activation(w_hi[:, slot], w_raw[:, slot], ACT.Copy).then_inc(hi_split, 1)

            def tick(at):
                if at.per or at.k + AHEAD < n_all:
                    split(at.plus(AHEAD))

            def full(u):
                act.wait_ge(small_full, u + 1)

            def turn_hi(u, bank, dst, gain, first):
                full(u)
                for i in range(2):
                    ins = act.activation(dst[:, first + i, :], small[:, bank, i * T:(i + 1) * T], ACT.Copy,
                                         scale=1.0 if gain is None else gain[:, first + i:first + i + 1])
                ins.then_inc(turned_hi, 1)

            g1 = columns[:, 5 * CC:5 * CC + KC]
            c_cqg = 5 * CC + KC + XC
            act.wait_ge(small_free_dve, 1)
            for r in range(8):
                if r == 4:
                    for n in range(AHEAD):
                        split(At(n))
                turn_hi(U_turn_x + r, (U_turn_x + r) % 2, act_hi, g1, 2 * r)
            for n in range(3 * KP):
                tick(At(n))
                if n == KP - 1:
                    done(act, At(n))
                    for t in range(NT):
                        act.activation(sq_flat[:, t * BANK:t * BANK + QL], A[:, t, 0:QL], ACT.Square,
                                       accum_out=ss[:, t:t + 1]).then_inc(squared, 1)
                if n == 2 * KP - 1:
                    done(act, At(n))
                    act.wait_ge(acc_free_dve, 1)
                    for t in range(NT):
                        act.activation(sq_flat[:, t * BANK:t * BANK + KVL], B[:, t, 0:KVL], ACT.Square,
                                       accum_out=ss[:, t:t + 1]).then_inc(squared, 1)
                    for r in range(2):
                        turn_hi(U_first + r, (U_first + r) % 2, cqt_hi, columns[:, c_cqg:c_cqg + 4], 2 * r)
                if n == 3 * KP - 1:
                    turn_hi(U_first + 2, U_first % 2, ckvt_hi, columns[:, c_cqg + 4:c_cqg + 6], 0)
                    act.wait_ge(sp_in, 1)
                    act.activation(sp[:, 2, :], sp[:, 1, :], ACT.Exp).then_inc(sp_exp, 1)
                    act.wait_ge(steps_landed, 48)
                    act.activation(sp[:, 7, 0:SH], steps_bc[:, 1, :], ACT.Exp).then_inc(sp_exp, 1)
            for n in range(4):
                tick(At(n_idx + n))
                if n % 2:
                    done(act, At(n_idx + n))
                    act.activation(qi_t[:, 4 * (n // 2):4 * (n // 2) + 4, :].rearrange("p c t -> p (c t)"),
                                   (B if n == 1 else A)[:, :, :].rearrange("p b n -> p (b n)"),
                                   ACT.Copy).then_inc(acc_free_act, 1)
            act.wait_ge(da_ready, 1)
            act.activation(da_split[:, 0:2, :], sp[:, 6, :].rearrange("p (t h) -> p t h", t=NT),
                           ACT.Copy).then_inc(da_hi, 1)
            for h in range(IDXH):
                full(U_idx + h)
                if h >= 2:
                    act.wait_ge(relu_used, h - 1)
                act.activation(relu[:, h % 2].rearrange("p t s -> p (t s)"), small[:, (U_idx + h) % 2, :],
                               ACT.Relu).then_inc(small_free_act, 1)

            g_qn, g_kn = columns[:, c_cqg + 6:c_cqg + 7], columns[:, c_cqg + 7:c_cqg + 8]
            with act.Fori(0, J) as j:
                def at(k):
                    return At(n_attn + k, j, J_P)

                def use(k):
                    return j * J_U + (U_attn + k)

                tick(at(0))
                tick(at(1))
                done(act, at(1))
                act.activation(sq_flat[:, :], B[:, :, :].rearrange("p t n -> p (t n)"), ACT.Square).then_inc(squared, 1)
                act.activation(q_raw[:, :, :, :].rearrange("p t h d -> p (t h d)"),
                               B[:, :, :].rearrange("p t n -> p (t n)"), ACT.Copy).then_inc(acc_free_act, 1)
                tick(at(2))
                for k in range(2):
                    if k:
                        tick(at(3))
                    done(act, at(2 + k))
                    ps = (A if k == 0 else B)[:, :, :].rearrange("p t (h n) -> p t h n", h=2)
                    for t in range(NT):
                        if k == 0 and t == 0:
                            act.wait_ge(sq_used, j * 2 + 1)
                        act.activation(sq[:, 4 * t + 2 * k:4 * t + 2 * k + 2, :], ps[:, t, :, 0:HD],
                                       ACT.Square).then_inc(squared, 1)
                    act.activation(kv_raw[:, :, 2 * k:2 * k + 2, :].rearrange("p t h d -> p t (h d)"),
                                   (A if k == 0 else B)[:, :, :], ACT.Copy).then_inc(acc_free_act, 1)
                for k in range(4, 7):
                    tick(at(k))
                for k, (dst, gain) in enumerate(((q_t, g_qn), (q_t, g_qn), (k_t, g_kn), (k_t, g_kn))):
                    full(use(k))
                    act.activation(dst[:, 2 * (k % 2):2 * (k % 2) + 2, :].rearrange("p h t -> p (h t)"),
                                   small[:, k % 2, :], ACT.Copy, scale=gain).then_inc(small_free_act, 1)
                tick(at(7))
                for h in range(4):
                    act.wait_ge(masked, j * 4 + (h + 1))
                    for t, (a, b) in enumerate(((0, P), (P, 3 * P))):
                        act.activation(prob[:, h, a:b], prob[:, h, a:b], ACT.Exp, bias=row_max[:, h, t:t + 1],
                                       accum_out=row_sum[:, h, t:t + 1]).then_inc(exped, 1)
                for k in range(8, 11):
                    tick(at(k))
                for r, u in ((0, 10), (1, 13)):
                    full(use(u))
                    act.activation(attn_hi[:, bass.ds(j * 4 + 2 * r, 2), :].rearrange("p h t -> p (h t)"),
                                   small[:, u % 2, :], ACT.Copy).then_inc(turned_hi, 1)
                tick(at(11))
                done(act, at(11))
                act.wait_ge(conv_g_ready, j + 1)
                for c in range(4):
                    act.activation(conv_acc[:, c, :], chan(A, c), ACT.Identity, bias=conv_g[:, TAPS, c:c + 1],
                                   scale=conv_g[:, TAPS - 1, c:c + 1]).then_inc(conv_biased, 1)
                act.wait_ge(acc_free_dve, j + (af_dve_j + 1))
                act.activation(bc_t[:, bass.ds(j * 4, 4), :], conv_acc[:, :, :], ACT.Silu).then_inc(conv_act, 1)
            with act.Fori(0, 2) as d:
                for k in range(2 * KP):
                    tick(At(n_ya + k, d, 2 * KP))
                    if k % KP == KP - 1:
                        done(act, At(n_ya + k, d, 2 * KP))
                        act.activation(ya[:, :, bass.ds(d * (2 * BANK) + k // KP * BANK, BANK)],
                                       (B if k < KP else A)[:, :, :], ACT.Copy).then_inc(acc_free_act, 1)

            with act.Fori(0, SG) as g:
                def at(k):
                    return At(n_ssm + k, g, G_P)

                def use(k):
                    return g * G_U + (U_ssm + k)

                for k in range(KP):
                    tick(at(k))
                done(act, at(KP - 1))
                act.wait_ge(group_ready, g * 5 + 1)
                for c in range(4):
                    act.activation(x_ch[:, c, :], chan(B, c), ACT.Identity, bias=conv_g[:, TAPS, c:c + 1],
                                   scale=conv_g[:, TAPS - 1, c:c + 1]).then_inc(conv_biased, 1)
                act.wait_ge(group_ready, g * 5 + 5)
                for k in range(4):
                    tick(at(KP + k))
                    for i in (2 * k, 2 * k + 1):
                        full(use(i))
                        act.activation(mix_t[:, i, 0:2 * P], small[:, i % 2, 0:2 * P], ACT.Exp,
                                       bias=per_head_g[:, 0, i:i + 1])
                        act.activation(mix_t[:, i, 2 * P:3 * P], small[:, i % 2, 2 * P:3 * P], ACT.Exp,
                                       bias=per_head_g[:, 1, i:i + 1]).then_inc(small_free_act, 1)
                    if k == 3:
                        act.wait_ge(acc_free_dve, g * 5 + (af_dve_g + 1))
                        act.activation(x_ch[:, :, :], x_ch[:, :, :], ACT.Silu).then_inc(conv_act, 1)
                for k in range(4, 6):
                    tick(at(KP + k))
                for t in range(NT):
                    full(use(8 + t))
                    act.activation(x_tok[:, t, :], small[:, t, :], ACT.Copy).then_inc(small_free_act, 1)
                for k in range(6, 8):
                    tick(at(KP + k))
                done(act, at(2 * KP - 1))
                act.activation(z_act[:, :, :], A[:, :, :], ACT.Silu).then_inc(acc_free_act, 1)
                tick(at(2 * KP))
                for t in range(NT):
                    act.wait_ge(y_gated, g * NT + (t + 1))
                    act.activation(y_skip[:, t, :], z_act[:, t, :], ACT.Square,
                                   accum_out=ss[:, t:t + 1]).then_inc(y_squared, 1)
                for k in range(1, 6):
                    tick(at(2 * KP + k))
                for r in range(2):
                    turn_hi(use(10 + r), r, yt_hi, gain_g, 2 * r)
                for k in range(6, 9):
                    tick(at(2 * KP + k))
                done(act, at(3 * KP - 1))
                act.activation(gates[:, :, bass.ds(g * BANK, BANK)], B[:, :, :], ACT.Sigmoid).then_inc(acc_free_act, 1)
                for k in range(1, 8):
                    tick(at(3 * KP + k))

            for r in range(8):
                turn_hi(U_late + r, r % 2, act_hi, None, 2 * r)
            for r in range(4):
                full(U_late + 8 + r)
                act.activation(keys_t[:, 4 * r:4 * r + 4, :].rearrange("p c k -> p (c k)"), small[:, r % 2, :],
                               ACT.Copy).then_inc(small_free_act, 1)
            with act.Fori(0, 2) as d:
                for k in range(2 * KP):
                    tick(At(n_wout + k, d, 2 * KP))
            act.wait_ge(acc_free_dve, af_dve_l + 4)
            for t in range(NT):
                act.activation(h2[:, t, :], x1[:, t, :], ACT.Square, accum_out=ss[:, t:t + 1]).then_inc(x1_squared, 1)
            for r in range(8):
                turn_hi(U_late + 12 + r, r % 2, act_hi, None, 2 * r)
            for k in range(4 * KP):
                tick(At(n_pq + k))
                b = k // KP
                if k % KP == KP - 1:
                    done(act, At(n_pq + k))
                    act.activation(qp[:, b % 2].rearrange("p c t -> p (c t)"),
                                   (A if b % 2 == 0 else B)[:, :, :].rearrange("p b n -> p (b n)"),
                                   ACT.Copy).then_inc(acc_free_act, 1)
                    for t in range(NT):
                        full(U_late + 20 + NT * b + t)
                        act.activation(sc[:, t, 4 * b:4 * b + 4, :].rearrange("p c k -> p (c k)"),
                                       small[:, t, :], ACT.Copy).then_inc(small_free_act, 1)
            def unit_scores(count, src):
                if not isinstance(count, int):
                    act.wait_ge(unit_ids, count)
                act.activation(sc_u[:, :, :], src, ACT.Copy).then_inc(unit_sc, 1)

            def unit_softmax(count, t):
                act.wait_ge(top_ready, count)
                act.activation(gate[:, t, :], pair_v[:, :], ACT.Exp, bias=g_max[:, 0:1],
                               accum_out=g_sum[:, t:t + 1]).then_inc(gate_exp, 1)

            unit_scores(0, sc[:, 0, 0:2, :])
            unit_softmax(1, 0)
            act.wait_ge(sc_padded, 1)
            with act.Fori(0, PH) as h:
                for t in range(NT):
                    unit_scores(h * NT + (t + 1), sc[:, 1 - t, bass.ds(h * 2 + 2 * t, 2), :])
                    act.wait_ge(slot_free, h * (2 * NT * PK) + (GATHERS + 2 * t * PK + PK))
                    act.activation(gelu[:, t, :], dots[:, t, :], ACT.Gelu).then_inc(gelued, 1)
                    unit_softmax(h * NT + (t + 2), 1 - t)

        @block.vector
        def _(dve):
            steps = Steps(dve, dve_step)

            def split(at):
                slot = at.k % RING
                dve.wait_ge(hi_split, at.count(1))
                dve.tensor_tensor(w_lo[:, slot], w_raw[:, slot], w_hi[:, slot].bitcast(F32),
                                  ALU.subtract).then_inc(lo_split, 1)

            def tick(at):
                if at.per or at.k + AHEAD < n_all:
                    split(at.plus(AHEAD))

            def step(instruction):
                steps.mark(instruction)
                steps.wait()

            def rsqrt(n, width):
                v, y, a, i = rq_v[:, 0:n], rstd[:, 0:n], rq_a[:, 0:n], rq_i[:, 0:n]
                step(dve.tensor_scalar(v, ss[:, 0:n], 1.0 / width, EPS, ALU.mult, ALU.add))
                step(dve.tensor_scalar(i, v.bitcast(I32), 1, None, ALU.logical_shift_right))
                step(dve.tensor_scalar(y.bitcast(I32), i, -1.0, RSQRT_MAGIC, ALU.mult, ALU.add))
                for _ in range(3):
                    step(dve.scalar_tensor_tensor(a, y, -0.5, y, ALU.mult, ALU.mult))
                    step(dve.tensor_tensor(a, a, v, ALU.mult))
                    step(dve.scalar_tensor_tensor(y, a, 1.5, y, ALU.add, ALU.mult))

            RSQRT_STEPS = 3 + 3 * 3

            def conv_taps(acc_sb, ps, biased):
                dve.wait_ge(conv_biased, biased)
                for back in range(1, TAPS):
                    for c in range(4):
                        o = acc_sb[:, c, back:T]
                        ins = dve.scalar_tensor_tensor(o, chan(ps, c)[:, 0:T - back],
                                                       conv_g[:, TAPS - 1 - back, c:c + 1], o, ALU.mult, ALU.add)
                        if back < TAPS - 1:
                            steps.mark(ins)
                    if back < TAPS - 1:
                        steps.wait()
                ins.then_inc(acc_free_dve, 1)

            CONV_STEPS = 4 * (TAPS - 2)

            def turn_lo(count, bank, hi, lo, gain, first):
                dve.wait_ge(turned_hi, count)
                for i in range(2):
                    ins = dve.scalar_tensor_tensor(
                        lo[:, first + i, :], small[:, bank, i * T:(i + 1) * T],
                        1.0 if gain is None else gain[:, first + i:first + i + 1],
                        hi[:, first + i, :].bitcast(F32), ALU.mult, ALU.subtract)
                ins.then_inc(small_free_dve, 1)

            for t in range(NT):
                dve.wait_ge(x_landed[t], 16)
                step(dve.tensor_tensor_reduce(x_junk[:, :], x_sb[:, t, :], x_sb[:, t, :], 1.0, 0.0, ALU.mult,
                                              ALU.add, ss[:, t:t + 1]))
            rsqrt(NT, D)
            for t in range(NT):
                dve.tensor_scalar(x_sb[:, t, :], x_sb[:, t, :], rstd[:, t:t + 1], None, ALU.mult).then_inc(xn_ready, 1)
            dve.wait_ge(small_full, 1)
            dve.tensor_copy(columns[:, :], small[:, 0, 0:296]).then_inc(small_free_dve, 1)
            dve.wait_ge(small_free_dve, 1)
            g1 = columns[:, 5 * CC:5 * CC + KC]
            c_cqg = 5 * CC + KC + XC
            for r in range(8):
                if r == 4:
                    for n in range(AHEAD):
                        split(At(n))
                turn_lo(r + 1, (U_turn_x + r) % 2, act_hi, act_lo, g1, 2 * r)

            for n in range(3 * KP):
                tick(At(n))
                if n == KP - 1:
                    dve.wait_ge(squared, NT)
                    rsqrt(NT, QL)
                    for t in range(NT):
                        ins = dve.tensor_scalar(cqn[:, t, :], A[:, t, 0:QL], rstd[:, t:t + 1], None, ALU.mult)
                    ins.then_inc(acc_free_dve, 1)
                if n == 2 * KP - 1:
                    dve.wait_ge(squared, 2 * NT)
                    rsqrt(NT, KVL)
                    for t in range(NT):
                        dve.tensor_scalar(ckvn[:, t, :], B[:, t, 0:KVL], rstd[:, t:t + 1], None, ALU.mult)
                    for t in range(NT):
                        dve.tensor_copy(kidx2[:, t], B[:, t, KVL:KVL + IDXD].unsqueeze(1).broadcast_to([P, 2, IDXD]))
                    for t in range(NT):
                        ins = dve.tensor_scalar(widx[:, t, :], B[:, t, KVL + IDXD:KVL + IDXD + IDXH],
                                                IDXH ** -0.5 * IDXD ** -0.5, None, ALU.mult)
                    ins.then_inc(acc_free_dve, 1)
                    for r in range(2):
                        turn_lo(8 + r + 1, (U_first + r) % 2, cqt_hi, cqt_lo, columns[:, c_cqg:c_cqg + 4], 2 * r)
                if n == 3 * KP - 1:
                    turn_lo(11, U_first % 2, ckvt_hi, ckvt_lo, columns[:, c_cqg + 4:c_cqg + 6], 0)
                    dve.wait_ge(small_full, U_first + 4)
                    dve.tensor_copy(ki_t[:, :], small[:, (U_first + 3) % 2, 0:T]).then_inc(small_free_dve, 1)
                    done(dve, At(n))
                    dve.wait_ge(steps_landed, 48)
                    for t in range(NT):
                        steps.mark(dve.tensor_tensor(sp[:, 0, t * SH:(t + 1) * SH], A[:, t, 0:SH], steps_bc[:, 0, :], ALU.add))
                    steps.wait()
                    dve.tensor_scalar(sp[:, 1, :], sp[:, 0, :], -1.0, None, ALU.mult).then_inc(acc_free_dve, 1)
                    dve.wait_ge(acc_free_dve, 3)
                    dve.tensor_tensor(sp[:, 1, :], sp[:, 1, :], sp[:, 0, :], ALU.min).then_inc(sp_in, 1)
                    dve.wait_ge(sp_exp, 2)
                    step(dve.tensor_scalar(sp[:, 3, :], sp[:, 2, :], 2.0, None, ALU.add))
                    step(dve.reciprocal(sp[:, 3, :], sp[:, 3, :]))
                    step(dve.tensor_tensor(sp[:, 3, :], sp[:, 3, :], sp[:, 2, :], ALU.mult))
                    step(dve.tensor_tensor(sp[:, 4, :], sp[:, 3, :], sp[:, 3, :], ALU.mult))
                    step(dve.tensor_scalar(sp[:, 5, :], sp[:, 4, :], 1.0 / 17, None, ALU.mult))
                    for k in (15, 13, 11, 9, 7, 5, 3):
                        step(dve.scalar_tensor_tensor(sp[:, 5, :], sp[:, 5, :], 1.0 / k, sp[:, 4, :], ALU.add, ALU.mult))
                    step(dve.scalar_tensor_tensor(sp[:, 5, :], sp[:, 5, :], 1.0, sp[:, 3, :], ALU.add, ALU.mult))
                    step(dve.tensor_scalar(sp[:, 5, :], sp[:, 5, :], 2.0, None, ALU.mult))
                    step(dve.tensor_scalar(sp[:, 0, :], sp[:, 0, :], 0.0, None, ALU.max))
                    dt = per_head[:, 2:4, :].rearrange("p t h -> p (t h)")
                    step(dve.tensor_tensor(dt, sp[:, 5, :], sp[:, 0, :], ALU.add))
                    for t in range(NT):
                        ins = dve.scalar_tensor_tensor(sp[:, 6, t * SH:(t + 1) * SH], sp[:, 7, 0:SH], -1.0,
                                                       per_head[:, 2 + t, :], ALU.mult, ALU.mult)
                    ins.then_inc(da_ready, 1)
            for n in range(4):
                tick(At(n_idx + n))
            dve.wait_ge(da_hi, 1)
            dve.tensor_tensor(da_split[:, 2:4, :], sp[:, 6, :].rearrange("p (t h) -> p t h", t=NT),
                              da_split[:, 0:2, :].bitcast(F32), ALU.subtract).then_inc(da_lo, 1)
            for h in range(IDXH):
                dve.wait_ge(small_free_act, h + 1)
                for t in range(NT):
                    w = widx[:, t, h:h + 1]
                    if h == 0:
                        ins = dve.tensor_scalar(score[:, t, :], relu[:, 0, t, :], w, None, ALU.mult)
                    else:
                        if t == 0:
                            dve.wait_ge(relu_used, h)
                        ins = dve.scalar_tensor_tensor(score[:, t, :], relu[:, h % 2, t, :], w, score[:, t, :],
                                                       ALU.mult, ALU.add)
                ins.then_inc(relu_used, 1)
            dve.wait_ge(small_full, U_cum + 1)
            dve.tensor_scalar(per_head[:, 0:2, :].rearrange("p t h -> p (t h)"), small[:, U_cum % 2, 0:NT * SH], -1.0, None,
                              ALU.mult).then_inc(small_free_dve, 1)
            dve.wait_ge(relu_used, IDXH)
            dve.wait_ge(consts, N_CONSTS)
            step(dve.tensor_tensor(score[:, :, :], score[:, :, :], causal[:, :, :], ALU.min))
            for t in range(NT):
                for _ in range(TOPK // 8):
                    step(dve.max(m8[:, :], score[:, t, :]))
                    step(dve.match_replace(score[:, t, :], m8[:, :], score[:, t, :], TAKEN))
            step(dve.tensor_scalar(keep[:, 0:P], score[:, 0, 0:P], -FAR * 1.1, NEG, ALU.is_gt, ALU.mult))
            step(dve.tensor_scalar(keep[:, P:3 * P], score[:, 1, :], -FAR * 1.1, NEG, ALU.is_gt, ALU.mult))
            step(dve.tensor_tensor(keep[:, :], keep[:, :], keep_c[:, :], ALU.min))

            with dve.Fori(0, J) as j:
                def at(k):
                    return At(n_attn + k, j, J_P)

                def use(k):
                    return j * J_U + (U_attn + k)

                steps.enter(j, RSQRT_STEPS + 4 * 2 + 4 + CONV_STEPS)
                tick(at(0))
                tick(at(1))
                tick(at(2))
                dve.wait_ge(squared, j * 5 + (2 * NT + 1))
                dve.tensor_reduce(ss[:, 0:8], sq[:, :, :], AX.X, ALU.add).then_inc(sq_used, 1)
                tick(at(3))
                dve.wait_ge(squared, j * 5 + (2 * NT + 5))
                dve.tensor_reduce(ss[:, 8:16], sq[:, :, :], AX.X, ALU.add).then_inc(sq_used, 1)
                dve.wait_ge(sq_used, j * 2 + 2)
                rsqrt(16, HD)
                tick(at(4))
                dve.wait_ge(acc_free_act, j * 3 + (af_act_j + 3))
                for t in range(NT):
                    dve.tensor_tensor(q_raw[:, t], q_raw[:, t],
                                      rstd[:, 4 * t:4 * t + 4].unsqueeze(2).broadcast_to([P, 4, HD]),
                                      ALU.mult).then_inc(qn_ready, 1)
                for t in range(NT):
                    dve.tensor_tensor(kv_raw[:, t, :, 0:HD], kv_raw[:, t, :, 0:HD],
                                      rstd[:, 8 + 4 * t:12 + 4 * t].unsqueeze(2).broadcast_to([P, 4, HD]),
                                      ALU.mult).then_inc(qn_ready, 1)
                for k in range(5, 8):
                    tick(at(k))
                for h in range(4):
                    dve.wait_ge(small_full, use(4 + h) + 1)
                    dve.scalar_tensor_tensor(prob[:, h, :], small[:, h % 2, 0:3 * P], HD ** -0.5, keep[:, :],
                                             ALU.mult, ALU.add).then_inc(small_free_dve, 1)
                    dve.wait_ge(small_free_dve, j * J_DVE + (sf_dve_j + h + 1))
                    for t, (a, b) in enumerate(((0, P), (P, 3 * P))):
                        steps.mark(dve.tensor_reduce(row_max[:, h, t:t + 1], prob[:, h, a:b], AX.X, ALU.max))
                    steps.wait()
                    dve.tensor_scalar(row_max[:, h, :], row_max[:, h, :], -1.0, None, ALU.mult).then_inc(masked, 1)
                tick(at(8))
                for h in range(4):
                    dve.wait_ge(exped, j * 8 + (2 * h + 2))
                    step(dve.reciprocal(row_inv[:, h, :], row_sum[:, h, :]))
                    for t, (a, b) in enumerate(((0, P), (P, 3 * P))):
                        ins = dve.tensor_scalar(prob[:, h, a:b], prob[:, h, a:b], row_inv[:, h, t:t + 1], None, ALU.mult)
                    ins.then_inc(probs, 1)
                tick(at(9))
                tick(at(10))
                for r in range(2):
                    for i in range(2):
                        u = 8 + 3 * r + i
                        dve.wait_ge(small_full, use(u) + 1)
                        dve.tensor_copy(prob_t[:, i, :], small[:, u % 2, 0:3 * P]).then_inc(small_free_dve, 1)
                    u = 10 + 3 * r
                    dve.wait_ge(turned_hi, j * 2 + (T_j + r + 1))
                    heads = bass.ds(j * 4 + 2 * r, 2)
                    dve.tensor_tensor(attn_lo[:, heads, :], small[:, u % 2, :].rearrange("p (h t) -> p h t", h=2),
                                      attn_hi[:, heads, :].bitcast(F32), ALU.subtract).then_inc(small_free_dve, 1)
                tick(at(11))
                conv_taps(conv_acc, A, j * 4 + 4)
                steps.leave(J)

            with dve.Fori(0, 2) as d:
                for k in range(2 * KP):
                    tick(At(n_ya + k, d, 2 * KP))

            with dve.Fori(0, SG) as g:
                def at(k):
                    return At(n_ssm + k, g, G_P)

                steps.enter(g, CONV_STEPS + RSQRT_STEPS)
                for k in range(KP):
                    tick(at(k))
                conv_taps(x_ch, B, g * 4 + (4 * J + 4))
                dve.wait_ge(cb_full, g + 1)
                dve.wait_ge(group_ready, g * 5 + 5)
                for k in range(4):
                    tick(at(KP + k))
                    for i in (2 * k, 2 * k + 1):
                        dve.wait_ge(small_free_act, g * G_ACT + (sf_act_g + i + 1))
                        dve.scalar_tensor_tensor(mix_t[:, i, 0:2 * P], mix_t[:, i, 0:2 * P], per_head_g[:, 2, i:i + 1],
                                                 pair_d[:, 0, 0:2 * P], ALU.mult, ALU.mult)
                        dve.scalar_tensor_tensor(mix_t[:, i, 2 * P:3 * P], mix_t[:, i, 2 * P:3 * P],
                                                 per_head_g[:, 3, i:i + 1], pair_d[:, 0, 2 * P:3 * P],
                                                 ALU.mult, ALU.mult).then_inc(mixed_t, 1)
                for k in range(4, 9):
                    tick(at(KP + k))
                dve.wait_ge(y_full, g + 1)
                dve.wait_ge(acc_free_act, g * 2 + (af_act_g + 1))
                for t in range(NT):
                    dve.wait_ge(skip_ready, g * NT + (t + 1))
                    dve.tensor_tensor(y_skip[:, t, :], y_skip[:, t, :], pair_d[:, t, :], ALU.add).then_inc(y_taken, 1)
                for t in range(NT):
                    dve.wait_ge(y_taken, g * NT + (t + 1))
                    dve.tensor_tensor(z_act[:, t, :], z_act[:, t, :], y_skip[:, t, :], ALU.mult).then_inc(y_gated, 1)
                for k in range(1, 3):
                    tick(at(2 * KP + k))
                dve.wait_ge(y_squared, g * NT + NT)
                rsqrt(NT, INNER // SG)
                for t in range(NT):
                    dve.tensor_scalar(z_act[:, t, :], z_act[:, t, :], rstd[:, t:t + 1], None,
                                      ALU.mult).then_inc(yn_ready, 1)
                for k in range(3, 6):
                    tick(at(2 * KP + k))
                for r in range(2):
                    turn_lo(g * 2 + (T_g + r + 1), r, yt_hi, yt_lo, gain_g, 2 * r)
                for k in range(6, 10):
                    tick(at(2 * KP + k))
                dve.wait_ge(yb_ready, 1)
                for d in range(4):
                    tick(at(3 * KP + 2 * d + 2) if d < 3 else at(G_P - 1))
                    done(dve, at(3 * KP + 2 * d + 1))
                    dve.wait_ge(acc_free_dve, g * 5 + (af_dve_g + 1 + d - 1 if d else af_dve_g))
                    ps = (A, B, A, pair_d)[d]
                    dve.tensor_tensor(yb[:, :, d * BANK:(d + 1) * BANK], yb[:, :, d * BANK:(d + 1) * BANK],
                                      ps[:, :, :], ALU.add).then_inc(acc_free_dve, 1)
                    if d < 2:
                        tick(at(3 * KP + 2 * d + 3))
                steps.leave(SG)

            dve.wait_ge(acc_free_act, af_act_l)
            dve.wait_ge(acc_free_dve, af_dve_l)

            def merge(d):
                cols = slice(d * BANK, (d + 1) * BANK)
                steps.mark(dve.tensor_tensor(ya[:, :, cols], ya[:, :, cols], gates[:, :, cols], ALU.mult))
                steps.mark(dve.tensor_tensor(yb[:, :, cols], yb[:, :, cols],
                                             gates[:, :, D + d * BANK:D + (d + 1) * BANK], ALU.mult))
                steps.wait()
                dve.tensor_tensor(ya[:, :, cols], ya[:, :, cols], yb[:, :, cols], ALU.add).then_inc(mixed, 1)

            merge(0)
            for d in range(4):
                if d < 3:
                    merge(d + 1)
                for r in (2 * d, 2 * d + 1):
                    turn_lo(T_l + r + 1, r % 2, act_hi, act_lo, None, 2 * r)
            dve.wait_ge(late_landed[0], 16 * NT)
            with dve.Fori(0, 2) as d:
                for k in range(2 * KP):
                    tick(At(n_wout + k, d, 2 * KP))
                    if k % KP == KP - 1:
                        done(dve, At(n_wout + k, d, 2 * KP))
                        cols = bass.ds(d * (2 * BANK) + k // KP * BANK, BANK)
                        dve.tensor_tensor(x1[:, :, cols], x1[:, :, cols], (A if k < KP else B)[:, :, :],
                                          ALU.add).then_inc(acc_free_dve, 1)
            dve.wait_ge(x1_squared, NT)
            rsqrt(NT, D)
            dve.wait_ge(late_landed[2], 16)

            def norm2(d):
                cols = slice(d * BANK, (d + 1) * BANK)
                for t in range(NT):
                    ins = dve.scalar_tensor_tensor(h2[:, t, cols], x1[:, t, cols], rstd[:, t:t + 1], gain2[:, cols],
                                                   ALU.mult, ALU.mult)
                ins.then_inc(h2_ready, 1)

            dve.wait_ge(acc_free_dve, af_dve_l + 4)
            norm2(0)
            for d in range(4):
                if d < 3:
                    norm2(d + 1)
                for r in (2 * d, 2 * d + 1):
                    turn_lo(T_l + 8 + r + 1, r % 2, act_hi, act_lo, None, 2 * r)
            for k in range(4 * KP):
                tick(At(n_pq + k))

            dve.sem_inc(slot_free, GATHERS)

            def top_experts(count, t):
                def wait():
                    steps.wait_apart(dve_passed)

                flat = cand[:, :, :].rearrange("p i j -> p (i j)")

                def best16(vals, idxs, tables):
                    for k in range(2):
                        e = slice(8 * k, 8 * k + 8)
                        for v, tb in zip(vals, tables):
                            steps.mark(dve.max(v[:, e], tb))
                        wait()
                        for v, ix, tb in zip(vals, idxs, tables):
                            steps.mark(dve.max_index(ix[:, e], v[:, e], tb))
                            if k == 0:
                                steps.mark(dve.match_replace(tb, v[:, e], tb, TAKEN))
                        wait()

                dve.wait_ge(unit_sc, count)
                if not isinstance(count, int):
                    dve.wait_ge(gate_exp, count - 1)
                steps.mark(dve.tensor_copy(part[:, 0, :], iota16[:, :]))
                wait()
                best16([top_v[:, c, :] for c in range(2)], [top_i[:, c, :] for c in range(2)],
                       [sc_u[:, c, :] for c in range(2)])
                steps.mark(dve.tensor_copy(top_f[:, :, :], top_i[:, :, :]))
                steps.mark(dve.tensor_tensor(cand[:, :, :], top_v[:, 0, :].unsqueeze(2).broadcast_to([P, PK, PK]),
                                             top_v[:, 1, :].unsqueeze(1).broadcast_to([P, PK, PK]), ALU.add))
                wait()
                best16([pair_v], [pair_i], [flat])
                dve.tensor_scalar(g_max[:, 0:1], pair_v[:, 0:1], -1.0, None, ALU.mult).then_inc(top_ready, 1)
                steps.mark(dve.tensor_scalar(pair_hl[:, 0, :], pair_i[:, :], 4, None, ALU.logical_shift_right))
                steps.mark(dve.tensor_scalar(pair_hl[:, 1, :], pair_i[:, :], PK - 1, None, ALU.bitwise_and))
                steps.wait()
                step(dve.tensor_copy(pair_f[:, :, :], pair_hl[:, :, :]))
                picks = (pick, cand)
                for c in range(2):
                    steps.mark(dve.tensor_tensor(picks[c][:, :, :], pair_f[:, c, :].unsqueeze(2).broadcast_to([P, PK, PK]),
                                                 iota16[:, :].unsqueeze(1).broadcast_to([P, PK, PK]), ALU.is_equal))
                steps.wait()
                for c in range(2):
                    steps.mark(dve.tensor_tensor(picks[c][:, :, :], picks[c][:, :, :],
                                                 top_f[:, c, :].unsqueeze(1).broadcast_to([P, PK, PK]), ALU.mult))
                steps.wait()
                for c in range(2):
                    steps.mark(dve.tensor_reduce(part[:, c, :], picks[c][:, :, :], AX.X, ALU.add))
                steps.wait()
                dve.scalar_tensor_tensor(eid[:, t, :], part[:, 0, :], float(NK), part[:, 1, :], ALU.mult,
                                         ALU.add).then_inc(unit_ids, 1)

            TOP_STEPS = 1 + (2 + 4 + 2 + 2) + 2 + (1 + 2 + 1 + 1) + 2 + 1 + 2 + 2 + 2
            top_experts(1, 0)
            with dve.Fori(0, PH) as h:
                steps.enter(h, NT * (TOP_STEPS + 1))
                used = 2 * NT * PK

                def landed(i):
                    dve.wait_ge(gathered[i % GATHERS], h * (used // GATHERS * 16) + (i // GATHERS + 1) * 16)

                for t in range(NT):
                    for k in range(PK):
                        i = 2 * t * PK + k
                        landed(i)
                        slot = slots[:, i % GATHERS, :]
                        dve.tensor_tensor_reduce(slot, slot, h2[:, t, :], 1.0, 0.0, ALU.mult, ALU.add,
                                                 dots[:, t, k:k + 1]).then_inc(slot_free, 1)
                    top_experts(h * NT + (t + 2), 1 - t)
                    dve.wait_ge(gate_exp, h * NT + (t + 1))
                    step(dve.reciprocal(g_inv[:, 0:1], g_sum[:, t:t + 1]))
                    dve.wait_ge(gelued, h * NT + (t + 1))
                    dve.scalar_tensor_tensor(share[:, t, :], gelu[:, t, :], g_inv[:, 0:1], gate[:, t, :], ALU.mult,
                                             ALU.mult).then_inc(shared, 1)
                    dve.wait_ge(shared, h * NT + (t + 1))
                    for k in range(PK):
                        i = (2 * t + 1) * PK + k
                        landed(i)
                        dve.wait_ge(slot_free, h * used + (GATHERS + i))
                        dve.scalar_tensor_tensor(x1[:, t, :], slots[:, i % GATHERS, :], share[:, t, k:k + 1],
                                                 x1[:, t, :], ALU.mult, ALU.add).then_inc(slot_free, 1)
                steps.leave(PH)

        @block.tensor
        def _(pe):
            def piece(at, width, acc_out, hi, lo, kc, first, last, channels):
                slot = at.k % RING
                pe.wait_ge(lo_split, at.count(1))
                for i in range(PIECE_KC):
                    start, stop = first and i == 0, last and i == PIECE_KC - 1
                    if channels:
                        for c in range(4):
                            o = chan(acc_out, c)
                            wh = w_hi[:, slot, i, c * P:(c + 1) * P]
                            wl = w_lo[:, slot, i, c * P:(c + 1) * P]
                            ah, al = hi[:, kc + i, :], lo[:, kc + i, :]
                            pe.matmul(o, wh, ah, start=start and c % 2 == 0, stop=False, skip_group_check=True)
                            pe.matmul(o, wh, al, start=False, stop=False, skip_group_check=True)
                            ins = pe.matmul(o, wl, ah, start=False, stop=stop, skip_group_check=True)
                    else:
                        for t in range(NT):
                            o = acc_out[:, t, 0:width]
                            wh, wl = w_hi[:, slot, i, 0:width], w_lo[:, slot, i, 0:width]
                            ah, al = hi[:, kc + i, t * P:(t + 1) * P], lo[:, kc + i, t * P:(t + 1) * P]
                            pe.matmul(o, ah, wh, start=start, stop=False)
                            pe.matmul(o, ah, wl, start=False, stop=False)
                            ins = pe.matmul(o, al, wh, start=False, stop=stop)
                ins.then_inc(w_used, 1)

            def pieces(at, which, width, acc_out, channels=False):
                for k in which:
                    piece(at.plus(k), width, acc_out, act_hi, act_lo, PIECE_KC * k, k == 0, k == KP - 1, channels)

            def transpose_to(out, in_, n=P):
                return pe.transpose(out, in_, ident[0:n, 0:n])

            def turn(bank, src, first):
                for i in range(2):
                    for t in range(NT):
                        ins = transpose_to(small[:, bank, i * T + t * P:i * T + (t + 1) * P],
                                           src[:, t, (first + i) * P:(first + i + 1) * P])
                ins.then_inc(small_full, 1)

            pe.wait_ge(rows_landed, 9 * 16)
            pe.wait_ge(consts, N_CONSTS)
            transpose_to(small[:, 0, 0:2 * CC], rows[0:2 * CC, 0, :], 2 * CC)
            transpose_to(small[:, 0, 2 * CC:4 * CC], rows[0:2 * CC, 1, :], 2 * CC)
            n_vec = 296 - 4 * CC
            transpose_to(small[:, 0, 4 * CC:296], rows[0:n_vec, 2, :], n_vec).then_inc(small_full, 1)
            pe.wait_ge(xn_ready, NT)
            for r in range(8):
                if r >= 1:
                    pe.wait_ge(small_free_dve, r)
                turn((U_turn_x + r) % 2, x_sb, 2 * r)
            pe.wait_ge(small_free_dve, S0_dve)
            pieces(At(0), range(KP), QL, A)
            pieces(At(KP), range(KP), KVL + IDXD + IDXH, B)
            pe.wait_ge(acc_free_dve, 1)
            for r in range(2):
                turn((U_first + r) % 2, cqn, 2 * r)
            pieces(At(2 * KP), range(KP), SH, A)
            pe.wait_ge(acc_free_dve, 2)
            pe.wait_ge(small_free_dve, S0_dve + 2)
            turn((U_first + 2) % 2, ckvn, 0)
            for t in range(NT):
                ins = transpose_to(small[:, (U_first + 3) % 2, t * P:(t + 1) * P],
                                   kidx2[:, t].rearrange("p a d -> p (a d)"))
            ins.then_inc(small_full, 1)
            for b, o in ((0, B), (1, A)):
                if b:
                    pe.wait_ge(acc_free_dve, 3)
                for k in range(2):
                    piece(At(n_idx + 2 * b + k), BANK, o, cqt_hi, cqt_lo, 2 * k, k == 0, k == 1, True)
            pe.wait_ge(small_free_dve, S0_dve + 4)
            pe.wait_ge(acc_free_act, 2)
            for h in range(IDXH):
                half = slice(IDXD * (h % 2), IDXD * (h % 2) + IDXD)
                if h >= 2:
                    pe.wait_ge(small_free_act, h - 1)
                for t in range(NT):
                    ins = pe.matmul(small[:, (U_idx + h) % 2, t * T:(t + 1) * T], qi_t[half, h // 2, t * P:(t + 1) * P],
                                    ki_t[half, :], start=True, stop=True)
                ins.then_inc(small_full, 1)
            pe.wait_ge(small_free_act, IDXH)
            pe.wait_ge(da_lo, 1)
            cum = small[:, U_cum % 2, 0:NT * SH].rearrange("p (t h) -> p t h", t=NT)
            pe.matmul(cum[:, 0, :], cum_rhs0[:, 0, :], da_split[:, 0, :], start=True, stop=False)
            pe.matmul(cum[:, 0, :], cum_rhs0[:, 0, :], da_split[:, 2, :], start=False, stop=True)
            pe.matmul(cum[:, 1, :], cum_rhs0[:, 1, :], da_split[:, 0, :], start=True, stop=False)
            pe.matmul(cum[:, 1, :], cum_rhs0[:, 1, :], da_split[:, 2, :], start=False, stop=False)
            pe.matmul(cum[:, 1, :], cum_rhs0[:, 0, :], da_split[:, 1, :], start=False, stop=False)
            pe.matmul(cum[:, 1, :], cum_rhs0[:, 0, :], da_split[:, 3, :], start=False, stop=True).then_inc(small_full, 1)

            with pe.Fori(0, J) as j:
                def at(k):
                    return At(n_attn + k, j, J_P)

                def act_free(n):
                    pe.wait_ge(small_free_act, j * J_ACT + (sf_act_j + n))

                def dve_free(n):
                    pe.wait_ge(small_free_dve, j * J_DVE + (sf_dve_j + n))

                pe.wait_ge(acc_free_act, j * 3 + af_act_j)
                for k in range(2):
                    piece(at(k), BANK, B, cqt_hi, cqt_lo, 2 * k, k == 0, k == 1, False)
                pe.wait_ge(acc_free_dve, j + af_dve_j)
                piece(at(2), BANK, A, ckvt_hi, ckvt_lo, 0, True, True, False)
                pe.wait_ge(acc_free_act, j * 3 + (af_act_j + 1))
                piece(at(3), BANK, B, ckvt_hi, ckvt_lo, 0, True, True, False)
                pe.wait_ge(acc_free_act, j * 3 + (af_act_j + 2))
                pieces(at(4), range(0, 2), BANK, A, True)
                for k, src in enumerate((q_raw, q_raw, kv_raw, kv_raw)):
                    if k == 0:
                        pe.wait_ge(qn_ready, j * 4 + 2)
                        act_free(0)
                        dve_free(0)
                    if k == 2:
                        pe.wait_ge(qn_ready, j * 4 + 4)
                    if k >= 2:
                        act_free(k - 1)
                    for i in range(2):
                        for t in range(NT):
                            ins = transpose_to(small[:, k % 2, i * T + t * P:i * T + (t + 1) * P],
                                               src[:, t, 2 * (k % 2) + i, 0:HD])
                    ins.then_inc(small_full, 1)
                pieces(at(4), range(2, 4), BANK, A, True)
                for h in range(4):
                    if h == 0:
                        act_free(4)
                    if h >= 2:
                        dve_free(h - 1)
                    o = small[:, h % 2, :]
                    pe.matmul(o[:, 0:P], q_t[:, h, 0:P], k_t[:, h, 0:P], start=True, stop=True)
                    pe.matmul(o[:, P:3 * P], q_t[:, h, P:2 * P], k_t[:, h, :], start=True, stop=True).then_inc(small_full, 1)
                pieces(at(4), range(4, 7), BANK, A, True)
                for r in range(2):
                    for i in range(2):
                        h, u = 2 * r + i, 8 + 3 * r + i
                        pe.wait_ge(probs, j * 4 + (h + 1))
                        dve_free(u - 4 - 1)
                        o = small[:, u % 2, :]
                        for b in range(3):
                            ins = transpose_to(o[:, b * P:(b + 1) * P], prob[:, h, b * P:(b + 1) * P])
                        ins.then_inc(small_full, 1)
                    u = 10 + 3 * r
                    dve_free(u - 4)
                    for i in range(2):
                        h = 2 * r + i
                        o = small[:, u % 2, i * T:(i + 1) * T]
                        pe.matmul(o, kv_raw[:, 0, h, HD:2 * HD], prob_t[:, i, 0:2 * P], start=True, stop=False)
                        ins = pe.matmul(o[:, P:2 * P], kv_raw[:, 1, h, HD:2 * HD], prob_t[:, i, 2 * P:3 * P],
                                        start=False, stop=True)
                    ins.then_inc(small_full, 1)
                pieces(at(4), range(7, 8), BANK, A, True)

            pe.wait_ge(small_free_dve, sf_dve_g)
            with pe.Fori(0, 2) as d:
                for b, o in ((0, B), (1, A)):
                    pe.wait_ge(acc_free_act, d * 2 + af_act_y)
                    if b:
                        pe.wait_ge(acc_free_dve, af_dve_y)
                    for k in range(KP):
                        piece(At(n_ya + b * KP + k, d, 2 * KP), BANK, o, attn_hi, attn_lo, 2 * k, k == 0, k == KP - 1, False)

            with pe.Fori(0, SG) as g:
                def at(k):
                    return At(n_ssm + k, g, G_P)

                def act_free(n):
                    pe.wait_ge(small_free_act, g * G_ACT + (sf_act_g + n))

                pe.wait_ge(acc_free_act, g * 2 + af_act_g)
                pe.wait_ge(acc_free_dve, g * 5 + (af_dve_g - 2))
                pieces(at(0), range(KP), BANK, B, True)
                pe.wait_ge(group_ready, g * 5 + 5)
                pe.wait_ge(acc_free_dve, g * 5 + af_dve_g)
                pe.matmul(pair_d[:, 0, 0:2 * P], bc_g[:, 0, 0:P], bc_g[:, 1, :], start=True, stop=True)
                pe.matmul(pair_d[:, 0, 2 * P:3 * P], bc_g[:, 0, P:2 * P], bc_g[:, 1, P:2 * P], start=True,
                          stop=True).then_inc(cb_full, 1)
                pe.wait_ge(small_free_dve, g * G_DVE + sf_dve_g)
                for k in range(KP):
                    pieces(at(KP), range(k, k + 1), BANK, A)
                    for i in ((2 * k, 2 * k + 1) if k < 4 else ()):
                        if i >= 2:
                            act_free(i - 1)
                        o = small[:, i % 2, 0:3 * P]
                        for part_, (ta, tb) in enumerate(((0, 1), (2, 3))):
                            pe.matmul(o, da_g[:, ta, i:i + 1].broadcast_to([P, P]),
                                      cum_rhs0[:, :, :].rearrange("p a b -> p (a b)"), start=part_ == 0, stop=False)
                            pe.matmul(o[:, P:3 * P], da_g[:, tb, i:i + 1].broadcast_to([P, P]),
                                      cum_rhs1[:, :, :].rearrange("p a b -> p (a b)"), start=False, stop=False)
                        pe.matmul(o[:, 0:P], ident_r[:, :], future_r[:, :], start=False, stop=False)
                        pe.matmul(o[:, 2 * P:3 * P], ident_r[:, :], future_r[:, :], start=False,
                                  stop=True).then_inc(small_full, 1)
                    if k == 5:
                        pe.wait_ge(conv_act, g + (J + 1))
                        for t in range(NT):
                            act_free(7 + t)
                            for c in range(4):
                                ins = transpose_to(small[:, t, c * P:(c + 1) * P], x_ch[:, c, t * P:(t + 1) * P])
                            ins.then_inc(small_full, 1)
                pe.wait_ge(mixed_t, g * GH + GH)
                act_free(10)
                for i in range(GH):
                    cols = slice(i * SHD, (i + 1) * SHD)
                    pe.matmul(pair_d[:, 0, cols], mix_t[:, i, 0:P], x_tok[:, 0, cols], start=True, stop=True)
                    pe.matmul(pair_d[:, 1, cols], mix_t[:, i, P:2 * P], x_tok[:, 0, cols], start=True, stop=False)
                    ins = pe.matmul(pair_d[:, 1, cols], mix_t[:, i, 2 * P:3 * P], x_tok[:, 1, cols], start=False, stop=True)
                ins.then_inc(y_full, 1)
                pe.wait_ge(acc_free_dve, g * 5 + (af_dve_g + 1))
                pieces(at(2 * KP), range(0, 6), BANK, B)
                pe.wait_ge(yn_ready, g * NT + NT)
                for r in range(2):
                    turn(r, z_act, 2 * r)
                pieces(at(2 * KP), range(6, 8), BANK, B)
                pe.wait_ge(small_free_dve, g * G_DVE + (sf_dve_g + 2))
                for d, o in enumerate((A, B, A, pair_d)):
                    if d < 2:
                        pe.wait_ge(acc_free_act, g * 2 + (af_act_g + 1 + d))
                    if d == 2:
                        pe.wait_ge(acc_free_dve, g * 5 + (af_dve_g + 2))
                    for k in range(2):
                        piece(at(3 * KP + 2 * d + k), BANK, o, yt_hi, yt_lo, 2 * k, k == 0, k == 1, False)

            for r in range(8):
                pe.wait_ge(mixed, r // 2 + 1)
                if r >= 2:
                    pe.wait_ge(small_free_dve, sf_dve_l + r - 1)
                turn(r % 2, ya, 2 * r)
            pe.wait_ge(late_landed[1], 16)
            pe.wait_ge(small_free_dve, sf_dve_l + 8)
            for r in range(4):
                if r >= 2:
                    pe.wait_ge(small_free_act, sf_act_l + r - 1)
                for c in range(4):
                    ins = transpose_to(small[:, r % 2, c * P:(c + 1) * P], keys[:, 4 * r + c, :])
                ins.then_inc(small_full, 1)
            with pe.Fori(0, 2) as d:
                for b, o in ((0, A), (1, B)):
                    pe.wait_ge(acc_free_dve, d * 2 + af_dve_l)
                    pieces(At(n_wout + b * KP, d, 2 * KP), range(KP), BANK, o)
            pe.wait_ge(small_free_act, sf_act_l + 4)
            for r in range(8):
                pe.wait_ge(h2_ready, r // 2 + 1)
                if r >= 2:
                    pe.wait_ge(small_free_dve, sf_dve_l + 8 + r - 1)
                turn(r % 2, h2, 2 * r)
            pe.wait_ge(small_free_dve, sf_dve_l + 16)
            pe.wait_ge(acc_free_dve, af_dve_l + 4)

            def key_scores(b):
                pe.wait_ge(acc_free_act, af_act_l + b + 1)
                for t in range(NT):
                    if b:
                        pe.wait_ge(small_free_act, sf_act_l + 4 + NT * (b - 1) + t + 1)
                    for c in range(4):
                        ins = pe.matmul(small[:, t, c * NK:(c + 1) * NK], qp[:, b % 2, c, t * P:(t + 1) * P],
                                        keys_t[:, 4 * b + c, :], start=True, stop=True)
                    ins.then_inc(small_full, 1)

            for b in range(4):
                if b >= 2:
                    pe.wait_ge(acc_free_act, af_act_l + b - 1)
                for k in range(KP):
                    pieces(At(n_pq + b * KP), range(k, k + 1), BANK, (A, B)[b % 2], True)
                    if k == 2 and b:
                        key_scores(b - 1)
            key_scores(3)


_INS = ["x", "g_norm1", "w_in", "g_cq", "g_ckv", "w_uq", "w_ukv", "g_qn", "g_kn", "w_iq", "w_o_attn",
        "conv_w", "conv_b", "dt_bias", "a_log", "d_skip", "g_ssm", "w_o_ssm", "w_out",
        "g_norm2", "w_peer_q", "peer_keys", "peer_u", "peer_v"]
_OUTS = [((1, 256, 2048), "float32")]


def kernel(**inputs):
    import numpy as _np
    import concourse.bacc as _bacc
    from concourse import mybir as _mybir
    from concourse.bass_utils import run_bass_kernel_spmd as _run

    nc = _bacc.Bacc("TRN2", target_bir_lowering=False, num_devices=1)
    arrays, args = {}, []
    for name in _INS:
        a = _np.ascontiguousarray(inputs[name])
        arrays[f"in_{name}_dram"] = a
        args.append(nc.dram_tensor(f"in_{name}_dram", a.shape, _mybir.dt.from_np(a.dtype), kind="ExternalInput").ap())
    for i, (shape, dtype) in enumerate(_OUTS):
        dt = _mybir.dt.from_np(_np.dtype(dtype))
        args.append(nc.dram_tensor(f"out_{i}_dram", shape, dt, kind="ExternalOutput").ap())
    hybrid_block(nc, *args)
    r = _run(nc, [arrays], core_ids=[0])
    got = tuple(r.results[0][f"out_{i}_dram"] for i in range(len(_OUTS)))
    return got[0]
```

```python
from contextlib import ExitStack

import concourse.bass as bass
from concourse import mybir

ALU = mybir.AluOpType
ACT = mybir.ActivationFunctionType
AX = mybir.AxisListType
F32 = mybir.dt.float32
F32R = mybir.dt.float32r
I32 = mybir.dt.int32
U32 = mybir.dt.uint32

P = 128
BANK = 512
PIECE_KC = 2
RING = 4
AHEAD = RING - 1
GATHERS = 8
EARLY = 4
NEG = -1.0e30
FAR = 3.0e38
TAKEN = -3.4e38
EPS = 1e-6
RSQRT_MAGIC = float(0x5F3759DF)


class Steps:

    def __init__(self, eng, sem):
        self.eng, self.sem, self.n, self.offset = eng, sem, 0, 0

    def mark(self, instruction):
        instruction.then_inc(self.sem, 1)
        self.n += 1
        return self.n

    def wait(self, n=None):
        self.eng.wait_ge(self.sem, self.offset + (self.n if n is None else n))

    def wait_apart(self, passed):
        self.wait()
        self.eng.sem_inc(passed, 1)

    def enter(self, index, per_trip, first=0):
        self.n -= first * per_trip
        self.start, self.per = self.n, per_trip
        self.offset, self.first = index * per_trip, first

    def leave(self, trips):
        assert self.n - self.start == self.per, (self.n - self.start, self.per)
        self.n, self.offset = self.start + self.per * (trips + self.first), 0


def hybrid_block(nc, x, g_norm1, w_in, g_cq, g_ckv, w_uq, w_ukv, g_qn, g_kn, w_iq, w_o_attn,
                 conv_w, conv_b, dt_bias, a_log, d_skip, g_ssm, w_o_ssm, w_out,
                 g_norm2, w_peer_q, peer_keys, peer_u, peer_v, out):
    T, D = x.shape[1], x.shape[2]
    NT = T // P
    KC = D // P
    QL, KVL = g_cq.shape[1], g_ckv.shape[1]
    HD = g_qn.shape[1]
    HEADS = w_uq.shape[2] // HD
    IDXH = 16
    IDXD = w_iq.shape[2] // IDXH
    TOPK = T // 4
    SH = dt_bias.shape[1]
    INNER = g_ssm.shape[1]
    SG = 8
    GH = SH // SG
    SHD = INNER // SH
    CONVD = conv_w.shape[2]
    CC = CONVD // P
    XC = INNER // P
    TAPS = conv_w.shape[1]
    PH = peer_keys.shape[1]
    NK = peer_keys.shape[3]
    PK = 16
    assert NT == 2 and D == 4 * BANK and HD == P and NK == P and SG * BANK == INNER

    c_cq = 0
    c_ckv = c_cq + QL
    c_kidx = c_ckv + KVL
    c_widx = c_kidx + IDXD
    c_z = c_widx + IDXH
    c_xbc = c_z + INNER
    c_bc = c_xbc + INNER
    c_dt = c_xbc + CONVD
    c_gate = c_dt + SH

    KP = KC // PIECE_KC
    n_first = 0
    n_idx = n_first + 2 * KP
    n_attn = n_idx + 4
    J = 4
    J_P = 2 + 2 + KP
    n_ya = n_attn + J * J_P
    n_ssm = n_ya + 4 * KP
    G_P = 4 * KP
    n_wout = n_ssm + SG * G_P
    n_pq = n_wout + 4 * KP
    n_all = n_pq + 4 * KP
    assert all(n % RING == 0 for n in (n_idx, n_attn, J_P, n_ya, n_ssm, G_P, n_wout, n_pq, n_all))

    IN2 = KVL + IDXD + IDXH + SH

    def width_of(at):
        return BANK if at.per or at.k >= n_idx else (QL, IN2)[(at.k - n_first) // KP]

    top = [(nc.sbuf_base + 63) // 64 * 64]
    most = [0]

    def sb(name, shape, dtype=F32):
        size = 4
        for s in shape[1:]:
            size *= s
        t = nc.alloc_sbuf_tensor_at(name, shape, dtype, offset=top[0])
        top[0] += (size + 31) // 32 * 32
        most[0] = max(most[0], top[0])
        return t

    ident = sb("ident", [P, P])
    ident_r = sb("ident_r", [P, P], F32R)
    cum_rhs0 = sb("cum_rhs0", [P, 3, P], F32R)
    cum_rhs1 = sb("cum_rhs1", [P, 2, P], F32R)
    future_r = sb("future_r", [P, P], F32R)
    tri = sb("tri", [P, P])
    ones = sb("ones", [P, P])
    iota16 = sb("iota16", [P, PK])
    iota_i = sb("iota_i", [P, PK], I32)
    COLS = 5 * CC + KC + XC + (QL + KVL) // P + 2 + KC
    columns = sb("columns", [P, COLS])
    steps_bc = sb("steps_bc", [P, 3, SH])
    rq_v = sb("rq_v", [P, 16])
    rq_i = sb("rq_i", [P, 16], I32)
    rq_a = sb("rq_a", [P, 16])
    ss = sb("ss", [P, 16])
    rstd = sb("rstd", [P, 16])
    per_head = sb("per_head", [P, 5, SH])
    da_split = sb("da_split", [P, 4, SH], F32R)
    r_act = top[0]
    act_hi = sb("act_hi", [P, KC, T], F32R)
    act_lo = sb("act_lo", [P, KC, T], F32R)
    w_raw = sb("w_raw", [P, RING, PIECE_KC, BANK])
    w_hi = sb("w_hi", [P, RING, PIECE_KC, BANK], F32R)
    w_lo = sb("w_lo", [P, RING, PIECE_KC, BANK], F32R)
    conv_g = sb("conv_g", [P, TAPS + 1, 4])
    r_bc = top[0]
    bc_t = sb("bc_t", [P, 2 * SG, T])
    r_after_bc = top[0]

    attn_hi = sb("attn_hi", [P, HEADS, T], F32R)
    attn_lo = sb("attn_lo", [P, HEADS, T], F32R)
    r_after_attn = top[0]
    cqt_hi = sb("cqt_hi", [P, QL // P, T], F32R)
    cqt_lo = sb("cqt_lo", [P, QL // P, T], F32R)
    ckvt_hi = sb("ckvt_hi", [P, KVL // P, T], F32R)
    ckvt_lo = sb("ckvt_lo", [P, KVL // P, T], F32R)
    r_qi = top[0]
    qi_hi = sb("qi_hi", [P, IDXH * IDXD // P, T], F32R)
    r_after_qi = top[0]
    ki_hi = sb("ki_hi", [P, T], F32R)
    ki_lo = sb("ki_lo", [P, T], F32R)
    score = sb("score", [P, NT, T])
    relu = sb("relu", [P, 2, NT, T])
    causal = sb("causal", [P, NT, T])
    keep_c = sb("keep_c", [P, 3 * P])
    keep = sb("keep", [P, 3 * P])
    m8 = sb("m8", [P, 8])
    sq = sb("sq", [P, 8, HD])
    prob = sb("prob", [P, 4, 3 * P])
    row_max = sb("row_max", [P, 4, NT])
    row_sum = sb("row_sum", [P, 4, NT])
    row_inv = sb("row_inv", [P, 4, NT])
    widx = sb("widx", [P, NT, IDXH])
    r_attn_end = top[0]
    top[0] = r_qi
    q_raw = sb("q_raw", [P, NT, 4, HD])
    prob_t = sb("prob_t", [P, 2, 3 * P])
    assert top[0] <= r_after_qi
    top[0] = r_attn_end
    kv_raw = sb("kv_raw", [P, NT, 4, 2 * HD])
    q_t = sb("q_t", [P, 4, T])
    k_t = sb("k_t", [P, 4, T])

    top[0] = r_after_bc
    x_sb = sb("x_sb", [P, NT, D])
    x_junk = sb("x_junk", [P, D])
    rows = sb("rows", [P, 3, P])
    cqn = sb("cqn", [P, NT, QL])
    assert top[0] <= r_after_attn
    top[0] = r_attn_end
    ckvn = sb("ckvn", [P, NT, KVL])
    kidx2 = sb("kidx2", [P, NT, 2, IDXD])
    sp = sb("sp", [P, 8, NT * SH])
    x_junk2 = sb("x_junk2", [P, D])
    qi_lo = sb("qi_lo", [P, IDXH * IDXD // P, T], F32R)

    top[0] = r_after_bc
    gate_b = sb("gate_b", [P, NT, D])
    yb = sb("yb", [P, NT, D])
    ya = sb("ya", [P, NT, D])
    r_after_y = top[0]
    gate_a = sb("gate_a", [P, NT, BANK // 2])
    bc_g = sb("bc_g", [P, 2, T])
    per_head_g = sb("per_head_g", [P, 5, GH])
    da_g = sb("da_g", [P, 4, GH], F32R)
    gain_g = sb("gain_g", [P, 4])
    mix_t = sb("mix_t", [P, GH, 3 * P])
    x_ch = sb("x_ch", [P, 4, T])
    x_tok = sb("x_tok", [P, NT, BANK])
    top[0] -= 2 * 4 * 4 * T
    y_skip = sb("y_skip", [P, NT, BANK])
    top[0] += 4 * NT * BANK
    z_act = sb("z_act", [P, NT, BANK])
    yt_hi = sb("yt_hi", [P, 4, T], F32R)
    yt_lo = sb("yt_lo", [P, 4, T], F32R)

    top[0] = r_after_y
    x1 = sb("x1", [P, NT, D])
    r_keys = top[0]
    keys = sb("keys", [P, 2 * PH, P])
    top[0] = r_keys
    h2 = sb("h2", [P, NT, D])
    keys_t = sb("keys_t", [P, 2 * PH, NK])
    r_late = top[0]
    top[0] = r_bc
    gain2 = sb("gain2", [P, D])
    sq2 = sb("sq2", [P, NT, BANK])
    top[0] -= 4 * NT * BANK
    qp = sb("qp", [P, 2, 4, T])
    top[0] = r_after_bc
    q_act_hi = sb("q_act_hi", [P, KC, T], F32R)
    q_act_lo = sb("q_act_lo", [P, KC, T], F32R)
    sc_first = sb("sc_first", [P, 2 * (PH + 1), NK])
    sc_u = sb("sc_u", [P, 2, NK])
    top_v = sb("top_v", [P, 2, PK])
    top_i = sb("top_i", [P, 2, PK], U32)
    top_f = sb("top_f", [P, 2, PK])
    cand = sb("cand", [P, PK, PK])
    pair_v = sb("pair_v", [P, PK])
    pair_i = sb("pair_i", [P, PK], U32)
    pair_hl = sb("pair_hl", [P, 2, PK], U32)
    pair_f = sb("pair_f", [P, 2, PK])
    pick = sb("pick", [P, PK, PK])
    part = sb("part", [P, 2, PK])
    eid = sb("eid", [P, NT, PK], U32)
    g_exp = sb("g_exp", [P, PK])
    g_max = sb("g_max", [P, 1])
    g_sum = sb("g_sum", [P, NT])
    g_inv = sb("g_inv", [P, 1])
    gate = sb("gate", [P, NT, PK])
    dots = sb("dots", [P, NT, PK])
    gelu = sb("gelu", [P, NT, PK])
    share = sb("share", [P, NT, PK])
    assert top[0] <= r_after_y
    top[0] = r_late
    sc = [sc_first, sb("sc_last", [P, 2 * (PH + 1), NK])]
    top[0] = r_act
    slots = sb("slots", [P, GATHERS, D])
    assert EARLY * D * 4 <= 2 * KC * T * 4
    assert top[0] <= r_bc and most[0] <= nc.sbuf_usable_end, most[0]

    with ExitStack() as ctx:
        def sem(name):
            return ctx.enter_context(nc.semaphore(name))

        acc = [ctx.enter_context(nc.psum_tensor(f"acc{i}", [P, 2, BANK], F32)) for i in "AB"]
        A, B = acc
        small = ctx.enter_context(nc.psum_tensor("small", [P, 2, BANK], F32))
        pair_d = ctx.enter_context(nc.psum_tensor("pair_d", [P, 2, BANK], F32))

        raw_landed = [sem(f"raw_landed{i}") for i in range(RING)]
        hi_split = sem("hi_split")
        lo_split = sem("lo_split")
        w_used = sem("w_used")
        acc_free_act = sem("acc_free_act")
        acc_free_dve = sem("acc_free_dve")
        small_full = sem("small_full")
        small_free_act = sem("small_free_act")
        small_free_dve = sem("small_free_dve")
        turned_hi = sem("turned_hi")
        rows_landed = sem("rows_landed")
        x_landed = [sem(f"x_landed{t}") for t in range(NT)]
        steps_landed = sem("steps_landed")
        consts = sem("consts")
        pool_step = sem("pool_step")
        dve_step = sem("dve_step")
        dve_passed = sem("dve_passed")
        pool_passed = sem("pool_passed")
        x_squared = sem("x_squared")
        x_rstd = sem("x_rstd")
        xn_ready = sem("xn_ready")
        squared = sem("squared")
        sp_in = sem("sp_in")
        sp_exp = sem("sp_exp")
        qi_split = sem("qi_split")
        da_ready = sem("da_ready")
        da_hi = sem("da_hi")
        da_lo = sem("da_lo")
        relu_used = sem("relu_used")
        conv_g_ready = sem("conv_g_ready")
        conv_biased = sem("conv_biased")
        conv_done = sem("conv_done")
        conv_act = sem("conv_act")
        sq_used = sem("sq_used")
        qn_ready = sem("qn_ready")
        masked = sem("masked")
        exped = sem("exped")
        probs = sem("probs")
        heads_full = sem("heads_full")
        group_ready = sem("group_ready")
        cb_full = sem("cb_full")
        mixed_t = sem("mixed_t")
        skip_ready = sem("skip_ready")
        y_full = sem("y_full")
        y_taken = sem("y_taken")
        y_gated = sem("y_gated")
        y_squared = sem("y_squared")
        yn_ready = sem("yn_ready")
        yb_ready = sem("yb_ready")
        gated_a = sem("gated_a")
        mixed = sem("mixed")
        rstd2_ready = sem("rstd2_ready")
        late_landed = [sem(f"late_landed{i}") for i in range(3)]
        x1_squared = sem("x1_squared")
        h2_ready = sem("h2_ready")
        sc_padded = sem("sc_padded")
        unit_sc = sem("unit_sc")
        unit_ids = sem("unit_ids")
        top_ready = sem("top_ready")
        gate_exp = sem("gate_exp")
        gathered = [sem(f"gathered{i}") for i in range(GATHERS)]
        slot_free = sem("slot_free")
        shared = sem("shared")
        gelued = sem("gelued")
        stored = sem("stored")

        U_turn_x = 1
        S0_dve = 1 + 8
        U_first = 9
        U_idx = U_first + 4
        U_cum = U_idx + IDXH
        U_attn = U_cum + 1
        J_AD = 3
        J_U, J_ACT, J_DVE = 12, 4, 8
        sf_act_j, sf_dve_j = IDXH, U_first + 4 + 1
        U_ssm = U_attn + J * J_U
        G_U, G_ACT, G_DVE = 12, 10, 2
        sf_act_g, sf_dve_g = sf_act_j + J * J_ACT, sf_dve_j + J * J_DVE
        U_late = U_ssm + SG * G_U
        sf_act_l, sf_dve_l = sf_act_g + SG * G_ACT, sf_dve_g + SG * G_DVE
        T_j = 8 + 3
        T_g = T_j + J * 2
        T_l = T_g + SG * 2
        af_dve_j, af_act_j = 3, 2
        af_dve_y, af_act_y = af_dve_j + J * J_AD, af_act_j + 3 * J
        af_dve_g, af_act_g = af_dve_y, af_act_y + 4
        af_dve_l, af_act_l = af_dve_g + 5 * SG, af_act_g + 2 * SG

        N_CONSTS = 7
        CQ_AT = (4, 5)
        FIRST_TOP = KP
        TOP_TICKS = 3
        X1_AT = (4, 5)
        SCORES_AT = 0

        UNIT_ROWS = 2 * PK

        def slot_of(i, early):
            return i % EARLY if early else (i + EARLY) % GATHERS

        def gate_loads(trips, k):
            gates = range(2 * KP, 3 * KP)
            return (trips * sum(m % RING == k % RING for m in gates)
                    + sum(m % RING == k % RING and m <= k for m in gates))

        class At:

            def __init__(self, k, index=0, per=0):
                self.k, self.index, self.per = k, index, per

            def plus(self, n):
                return At(self.k + n, self.index, self.per)

            def count(self, add=0):
                return self.index * self.per + (self.k + add) if self.per else self.k + add

            def landed(self):
                loads, per = self.k // RING + 1, self.per // RING
                loads += min(max(self.k // RING + 1 - KP // RING, 0), KP // RING)
                if self.per == G_P:
                    trip, k = divmod(self.k - n_ssm, G_P)
                    loads += gate_loads(trip, k)
                    per += gate_loads(1, 0)
                elif self.k >= n_wout:
                    loads += gate_loads(SG, 0)
                return self.index * (per * 16) + loads * 16 if self.per else loads * 16

        sq_flat = sq[:, :, :].rearrange("p a b -> p (a b)")

        def chan(ps, c):
            return ps[:, c // 2, c % 2 * T:(c % 2 + 1) * T]

        def done(eng, at):
            eng.wait_ge(w_used, at.count(1))

        block = ctx.enter_context(nc.Block())

        @block.sync
        def _(sp):
            for t in range(NT):
                sp.dma_start(x_sb[:, t, :], x[0, t * P:(t + 1) * P, :]).then_inc(x_landed[t], 16)

            def piece(n, local, w, row0, col0, width=BANK):
                slot = local % RING
                if not (isinstance(n, int) and n < RING):
                    sp.wait_ge(lo_split, n - RING + 1)
                src = w[0, bass.ds(row0, PIECE_KC * P), bass.ds(col0, width)]
                sp.dma_start(w_raw[:, slot, :, 0:width],
                             src.rearrange("(k p) n -> p k n", p=P)).then_inc(raw_landed[slot], 16)

            def full_block(n, local, w, col0, width=BANK):
                for j in range(KP):
                    piece(n + j, local + j, w, j * PIECE_KC * P, col0, width)

            def gate_block(n, local, g):
                for j in range(KP):
                    slot = (local + j) % RING
                    sp.wait_ge(lo_split, n + j - RING + 1)
                    half = BANK // 2
                    for b in range(2):
                        src = w_in[0, j * PIECE_KC * P:(j + 1) * PIECE_KC * P,
                                   bass.ds(g * half + (c_gate + b * D), half)]
                        sp.dma_start(w_raw[:, slot, :, b * half:(b + 1) * half],
                                     src.rearrange("(k p) n -> p k n", p=P)).then_inc(raw_landed[slot], 16)

            full_block(n_first, 0, w_in, c_cq, QL)
            for j in range(KP):
                n = n_first + KP + j
                piece(n, n, w_in, j * PIECE_KC * P, c_ckv, IN2 - SH)
                src = w_in[0, j * PIECE_KC * P:(j + 1) * PIECE_KC * P, c_dt:c_dt + SH]
                sp.dma_start(w_raw[:, n % RING, :, IN2 - SH:IN2],
                             src.rearrange("(k p) n -> p k n", p=P)).then_inc(raw_landed[n % RING], 16)
            for i, v in enumerate((dt_bias, a_log, d_skip)):
                sp.dma_start(steps_bc[:, i, :], v[0:1, :].broadcast_to([P, SH])).then_inc(steps_landed, 16)
            for b in range(2):
                for j in range(2):
                    piece(n_idx + 2 * b + j, 2 * b + j, w_iq, j * PIECE_KC * P, b * BANK)
            with sp.Fori(0, J) as j:
                n = j * J_P + n_attn
                for k in range(2):
                    piece(n + k, k, w_uq, k * PIECE_KC * P, j * BANK)
                for k in range(2):
                    piece(n + 2 + k, 2 + k, w_ukv, 0, j * (2 * BANK) + k * BANK)
                full_block(n + 4, 4, w_in, j * BANK + c_bc)
            with sp.Fori(0, 2) as d:
                for k in range(2):
                    full_block(d * (2 * KP) + (n_ya + k * KP), k * KP, w_o_attn, d * (2 * BANK) + k * BANK)
            with sp.Fori(0, SG) as g:
                n = g * G_P + n_ssm
                full_block(n, 0, w_in, g * BANK + c_xbc)
                full_block(n + KP, KP, w_in, g * BANK + c_z)
                gate_block(n + 2 * KP, 2 * KP, g)
                for d in range(4):
                    for k in range(2):
                        piece(n + 3 * KP + 2 * d + k, 2 * d + k, w_o_ssm, g * BANK + k * PIECE_KC * P, d * BANK)
            for base, w in ((n_wout, w_out), (n_pq, w_peer_q)):
                with sp.Fori(0, 2) as d:
                    for k in range(2):
                        full_block(d * (2 * KP) + (base + k * KP), k * KP, w, d * (2 * BANK) + k * BANK)
            sp.wait_ge(slot_free, PH * NT * UNIT_ROWS)
            for t in range(NT):
                sp.dma_start(out[0, t * P:(t + 1) * P, :], x1[:, t, :]).then_inc(stored, 16)
            sp.wait_ge(stored, 16 * NT)

        @block.gpsimd
        def _(pool):
            steps = Steps(pool, pool_step)

            def select(t, pattern, base, channel, fill):
                steps.wait()
                return pool.affine_select(out=t, in_=t, pattern=pattern, compare_op=ALU.is_ge, fill=fill,
                                          base=base, channel_multiplier=channel)

            steps.mark(pool.memset(ident[:, :], 0.0))
            steps.mark(pool.memset(tri[:, :], 1.0))
            steps.mark(pool.memset(ones[:, :], 1.0))
            steps.mark(pool.memset(causal[:, :, :], FAR))
            steps.mark(pool.memset(keep_c[:, :], 0.0))
            steps.mark(pool.memset(keep[:, 0:P], 0.0))
            steps.mark(pool.iota(iota_i[:, :], pattern=[[1, PK]], base=0, channel_multiplier=0))
            steps.wait()
            steps.mark(pool.affine_select(out=ident[:, :], in_=ident[:, :], compare_op=ALU.not_equal, fill=1.0,
                                          base=0, pattern=[[-1, P]], channel_multiplier=1))
            steps.mark(select(tri[:, :], [[1, P]], 0, -1, 0.0))
            for t in range(NT):
                steps.mark(select(causal[:, t, :], [[-1, T]], t * P, 1, -FAR))
            steps.mark(select(keep_c[:, 0:P], [[-1, P]], 0, 1, NEG))
            steps.mark(select(keep_c[:, P:3 * P], [[-1, T]], P, 1, NEG))
            steps.mark(select(keep[:, 0:P], [[1, P]], 0, -1, NEG))
            steps.mark(pool.tensor_copy(iota16[:, :], iota_i[:, :]))
            steps.wait()
            pool.tensor_copy(ident_r[:, :], ident[:, :]).then_inc(consts, 1)
            for i, t in enumerate((tri, ones, ones)):
                pool.tensor_copy(cum_rhs0[:, i, :], t[:, :]).then_inc(consts, 1)
            for i in range(2):
                pool.tensor_copy(cum_rhs1[:, i, :], tri[:, :]).then_inc(consts, 1)
            pool.tensor_copy(future_r[:, :], keep[:, 0:P]).then_inc(consts, 1)

            taps = columns[:, 0:(TAPS + 1) * CC].rearrange("p (k c) -> p k c", c=CC)
            pool.wait_ge(small_free_dve, 1)
            with pool.Fori(0, J) as j:
                pool.wait_ge(acc_free_dve, j * J_AD + af_dve_j)
                pool.tensor_copy(conv_g[:, :, :], taps[:, :, bass.ds(j * 4 + XC, 4)]).then_inc(conv_g_ready, 1)
            pool.wait_ge(steps_landed, 48)
            pool.wait_ge(da_lo, 1)
            pool.wait_ge(small_free_dve, sf_dve_j)
            steps.mark(pool.tensor_copy(per_head[:, 4, :], steps_bc[:, 2, :]))
            steps.wait()
            pool.wait_ge(conv_act, 4)
            pool.wait_ge(acc_free_act, af_act_g)
            pool.memset(yb[:, :, :], 0.0).then_inc(yb_ready, 1)
            bc_pairs = bc_t[:, :, :].rearrange("p (k g) t -> p k g t", k=2)
            with pool.Fori(0, SG) as g:
                pool.wait_ge(small_free_dve, g * G_DVE + sf_dve_g)
                pool.tensor_copy(conv_g[:, :, :], taps[:, :, bass.ds(g * 4, 4)]).then_inc(group_ready, 1)
                pool.tensor_copy(bc_g[:, :, :], bc_pairs[:, :, bass.ds(g, 1), :].rearrange("p k g t -> p k (g t)")).then_inc(group_ready, 1)
                pool.tensor_copy(per_head_g[:, :, :], per_head[:, :, bass.ds(g * GH, GH)]).then_inc(group_ready, 1)
                pool.tensor_copy(da_g[:, :, :], da_split[:, :, bass.ds(g * GH, GH)].bitcast(F32)).then_inc(group_ready, 1)
                pool.tensor_copy(gain_g[:, :], columns[:, bass.ds(g * 4 + (5 * CC + KC), 4)]).then_inc(group_ready, 1)
                pool.wait_ge(group_ready, g * 5 + 5)
                pool.wait_ge(small_free_act, g * G_ACT + (sf_act_g + G_ACT))
                for t in range(NT):
                    pool.tensor_tensor(y_skip[:, t, :].rearrange("p (h c) -> p h c", c=SHD),
                                       x_tok[:, t, :].rearrange("p (h c) -> p h c", c=SHD),
                                       per_head_g[:, 4, :].unsqueeze(2).broadcast_to([P, GH, SHD]),
                                       ALU.mult).then_inc(skip_ready, 1)
                pool.wait_ge(acc_free_act, g * 2 + (af_act_g + 2))
                ya_cols = ya[:, :, bass.ds(g * (BANK // 2), BANK // 2)]
                pool.tensor_tensor(ya_cols, ya_cols, gate_a[:, :, :], ALU.mult).then_inc(gated_a, 1)

            pool.wait_ge(gated_a, SG)
            for d in range(4):
                cols = slice(d * BANK, (d + 1) * BANK)
                pool.wait_ge(acc_free_dve, af_dve_l - 4 + d + 1)
                steps.mark(pool.tensor_tensor(yb[:, :, cols], yb[:, :, cols], gate_b[:, :, cols], ALU.mult))
                steps.wait()
                pool.tensor_tensor(ya[:, :, cols], ya[:, :, cols], yb[:, :, cols], ALU.add).then_inc(mixed, 1)
            pool.wait_ge(small_free_dve, sf_dve_l)
            pool.wait_ge(acc_free_dve, af_dve_l)
            for t in range(NT):
                pool.dma_start(x1[:, t, :], x[0, t * P:(t + 1) * P, :]).then_inc(late_landed[0], 16)
            pool.dma_start(keys[:, :, :], peer_keys[0].rearrange("h c k d -> k (h c) d")).then_inc(late_landed[1], 16)
            pool.dma_start(gain2[:, :], g_norm2[0:1, :].broadcast_to([P, D])).then_inc(late_landed[2], 16)
            pool.wait_ge(small_free_dve, sf_dve_l + 8)
            for t in range(NT):
                pool.memset(sc[t][:, 2 * PH:2 * PH + 2, :], 0.0).then_inc(sc_padded, 1)

            def gather(h, t, early):
                pool.wait_ge(unit_ids, h * NT + (t + 1))
                for half, table in enumerate((peer_u[0], peer_v[0])):
                    for k in range(PK):
                        i = (2 * t + half) * PK + k
                        if not early:
                            pool.wait_ge(slot_free, h * UNIT_ROWS * NT + (i - GATHERS + 1))
                            pool.sem_inc(pool_passed, 1)
                        elif i >= EARLY:
                            pool.wait_ge(slot_free, i - EARLY + 1)
                            pool.sem_inc(pool_passed, 1)
                        slot = slot_of(i, early)
                        pool.indirect_dma_start(slots[:, slot, :], None, table,
                                                bass.IndirectOffsetOnAxis(ap=eid[:, t, k:k + 1], axis=0)
                                                ).then_inc(gathered[slot], 16)

            pool.wait_ge(w_used, n_pq)
            for t in range(NT):
                gather(0, t, True)
            pool.wait_ge(w_used, n_all)
            with pool.Fori(1, PH) as h:
                for t in range(NT):
                    gather(h, t, False)

        @block.scalar
        def _(act):
            def split(at):
                slot = at.k % RING
                act.wait_ge(raw_landed[slot], at.landed())
                if at.per or at.k >= RING:
                    act.wait_ge(w_used, at.count(1 - RING))
                w = width_of(at)
                act.activation(w_hi[:, slot, :, 0:w], w_raw[:, slot, :, 0:w], ACT.Copy).then_inc(hi_split, 1)

            def tick(at):
                if at.per or at.k + AHEAD < n_all:
                    split(at.plus(AHEAD))

            def full(u):
                act.wait_ge(small_full, u + 1)

            def turn_hi(u, bank, dst, gain, first):
                full(u)
                for i in range(2):
                    ins = act.activation(dst[:, first + i, :], small[:, bank, i * T:(i + 1) * T], ACT.Copy,
                                         scale=1.0 if gain is None else gain[:, first + i:first + i + 1])
                ins.then_inc(turned_hi, 1)

            def vec(i, row, v):
                n = v.shape[0]
                act.dma_start(rows[row:row + n, i, :], v).then_inc(rows_landed, 16)

            def by_rows(v):
                return v.rearrange("a (c p) -> (a c) p", p=P)

            taps = conv_w[0].rearrange("k (c p) -> (k c) p", p=P)
            vec(0, 0, taps[0:2 * CC, :])
            vec(1, 0, taps[2 * CC:4 * CC, :])
            row = 0
            for v in (conv_b, g_norm1, g_ssm, g_cq, g_ckv, g_qn, g_kn, g_norm2):
                vec(2, row, by_rows(v))
                row += v.shape[1] // P
            act.wait_ge(consts, N_CONSTS)
            act.activation(ss[:, 15:16], ones[:, 0:1], ACT.Square)
            act.wait_ge(x_landed[1], 16)
            act.activation(x_junk2[:, :], x_sb[:, 1, :], ACT.Square, accum_out=ss[:, 1:2]).then_inc(x_squared, 1)
            act.wait_ge(x_rstd, 1)
            act.activation(x_sb[:, 1, :], x_sb[:, 1, :], ACT.Copy, scale=rstd[:, 1:2]).then_inc(xn_ready, 1)
            def x1_turn(r):
                if r % 2 == 0:
                    d = r // 2
                    act.wait_ge(acc_free_dve, af_dve_l + d + 1)
                    for t in range(NT):
                        act.activation(sq2[:, t, :], x1[:, t, d * BANK:(d + 1) * BANK], ACT.Square,
                                       accum_out=ss[:, 8 + 4 * t + d:9 + 4 * t + d]).then_inc(x1_squared, 1)
                turn_hi(U_late + 12 + r, r % 2, q_act_hi, g2, 2 * r)

            g2 = columns[:, COLS - KC:COLS]
            g1 = columns[:, 5 * CC:5 * CC + KC]
            c_cqg = 5 * CC + KC + XC
            act.wait_ge(small_free_dve, 1)
            for r in range(2):
                turn_hi(U_turn_x + r, (U_turn_x + r) % 2, act_hi, g1, 2 * r)
            for n in range(AHEAD):
                split(At(n))
            for n in range(2 * KP + 4):
                tick(At(n))
                if n + 2 < KP:
                    turn_hi(U_turn_x + n + 2, (U_turn_x + n) % 2, act_hi, g1, 2 * (n + 2))
                if n == KP - 1:
                    done(act, At(n))
                    for t in range(NT):
                        act.activation(sq_flat[:, t * BANK:t * BANK + QL], A[:, t, 0:QL], ACT.Square,
                                       accum_out=ss[:, t:t + 1]).then_inc(squared, 1)
                if n - KP in CQ_AT:
                    r = CQ_AT.index(n - KP)
                    turn_hi(U_first + r, (U_first + r) % 2, cqt_hi, columns[:, c_cqg:c_cqg + 4], 2 * r)
                if n == 2 * KP - 1:
                    done(act, At(n))
                    act.wait_ge(acc_free_dve, 1)
                    for t in range(NT):
                        act.activation(sq_flat[:, t * BANK:t * BANK + KVL], B[:, t, 0:KVL], ACT.Square,
                                       accum_out=ss[:, t:t + 1]).then_inc(squared, 1)
                if n == n_idx:
                    act.wait_ge(sp_in, 1)
                    act.activation(sp[:, 2, :], sp[:, 1, :], ACT.Exp).then_inc(sp_exp, 1)
                    act.wait_ge(steps_landed, 48)
                    act.activation(sp[:, 7, 0:SH], steps_bc[:, 1, :], ACT.Exp).then_inc(sp_exp, 1)
                if n in (n_idx + 1, n_idx + 3):
                    b = (n - n_idx) // 2
                    done(act, At(n))
                    act.activation(qi_hi[:, 4 * b:4 * b + 4, :].rearrange("p c t -> p (c t)"),
                                   (A, pair_d)[b][:, :, :].rearrange("p b n -> p (b n)"),
                                   ACT.Copy).then_inc(acc_free_act, 1)
            turn_hi(U_first + 2, U_first % 2, ckvt_hi, columns[:, c_cqg + 4:c_cqg + 6], 0)
            for h in range(IDXH):
                full(U_idx + h)
                if h >= 2:
                    act.wait_ge(relu_used, h - 1)
                act.activation(relu[:, h % 2].rearrange("p t s -> p (t s)"), small[:, (U_idx + h) % 2, :],
                               ACT.Relu).then_inc(small_free_act, 1)
                if h == 13:
                    act.wait_ge(da_ready, 1)
                    act.activation(da_split[:, 0:2, :], sp[:, 6, :].rearrange("p (t h) -> p t h", t=NT),
                                   ACT.Copy).then_inc(da_hi, 1)
            for k in range(2):
                tick(At(n_attn + k))

            q_gain, k_gain = columns[:, c_cqg + 6:c_cqg + 7], columns[:, c_cqg + 7:c_cqg + 8]
            with act.Fori(0, J) as j:
                def at(k):
                    return At(n_attn + k, j, J_P)

                def use(k):
                    return j * J_U + (U_attn + k)

                done(act, at(1))
                act.wait_ge(acc_free_dve, j * J_AD + (af_dve_j - 1))
                act.activation(sq_flat[:, :], B[:, :, :].rearrange("p t n -> p (t n)"), ACT.Square).then_inc(squared, 1)
                act.activation(q_raw[:, :, :, :].rearrange("p t h d -> p (t h d)"),
                               B[:, :, :].rearrange("p t n -> p (t n)"), ACT.Copy).then_inc(acc_free_act, 1)
                for k in range(2):
                    tick(at(2 + k))
                    done(act, at(2 + k))
                    ps = (A if k == 0 else B)[:, :, :].rearrange("p t (h n) -> p t h n", h=2)
                    for t in range(NT):
                        if k == 0 and t == 0:
                            act.wait_ge(sq_used, j * 2 + 1)
                        act.activation(sq[:, 4 * t + 2 * k:4 * t + 2 * k + 2, :], ps[:, t, :, 0:HD],
                                       ACT.Square).then_inc(squared, 1)
                    act.activation(kv_raw[:, :, 2 * k:2 * k + 2, :].rearrange("p t h d -> p t (h d)"),
                                   (A if k == 0 else B)[:, :, :], ACT.Copy).then_inc(acc_free_act, 1)
                for k, (dst, gain) in enumerate(((q_t, q_gain), (q_t, q_gain), (k_t, k_gain), (k_t, k_gain))):
                    if k % 2 == 0:
                        tick(at(4 + k))
                        tick(at(5 + k))
                    full(use(k))
                    act.activation(dst[:, 2 * (k % 2):2 * (k % 2) + 2, :].rearrange("p h t -> p (h t)"),
                                   small[:, k % 2, :], ACT.Copy, scale=gain).then_inc(small_free_act, 1)
                for h in range(4):
                    if h % 2 == 0:
                        tick(at(8 + h // 2))
                    act.wait_ge(masked, j * 4 + (h + 1))
                    for t, (a, b) in enumerate(((0, P), (P, 3 * P))):
                        act.activation(prob[:, h, a:b], prob[:, h, a:b], ACT.Exp, bias=row_max[:, h, t:t + 1],
                                       accum_out=row_sum[:, h, t:t + 1]).then_inc(exped, 1)
                tick(at(10))
                tick(at(11))
                for r in range(2):
                    act.wait_ge(heads_full, j * 2 + (r + 1))
                    act.activation(attn_hi[:, bass.ds(j * 4 + 2 * r, 2), :].rearrange("p h t -> p (h t)"),
                                   A[:, r, :], ACT.Copy).then_inc(turned_hi, 1)
                done(act, at(11))
                act.wait_ge(conv_g_ready, j + 1)
                for c in range(4):
                    act.activation(bc_t[:, bass.ds(j * 4 + c, 1), :].rearrange("p c t -> p (c t)"), chan(pair_d, c),
                                   ACT.Identity, bias=conv_g[:, TAPS, c:c + 1],
                                   scale=conv_g[:, TAPS - 1, c:c + 1]).then_inc(conv_biased, 1)
                tick(at(J_P))
                tick(at(J_P + 1))
            for k in range(4 * KP):
                if k >= 2:
                    tick(At(n_ya + k))
                if k % KP == KP - 1:
                    b = k // KP
                    done(act, At(n_ya + k))
                    act.activation(ya[:, :, b * BANK:(b + 1) * BANK],
                                   (B, A)[b % 2][:, :, :], ACT.Copy).then_inc(acc_free_act, 1)

            act.wait_ge(acc_free_dve, af_dve_y)
            for c in range(4):
                act.activation(bc_t[:, 4 * c:4 * c + 4, :], bc_t[:, 4 * c:4 * c + 4, :], ACT.Silu).then_inc(conv_act, 1)

            with act.Fori(0, SG) as g:
                def at(k):
                    return At(n_ssm + k, g, G_P)

                def use(k):
                    return g * G_U + (U_ssm + k)

                for k in range(KP):
                    tick(at(k))
                done(act, at(KP - 1))
                act.wait_ge(group_ready, g * 5 + 1)
                for c in range(4):
                    act.activation(x_ch[:, c, :], chan(B, c), ACT.Identity, bias=conv_g[:, TAPS, c:c + 1],
                                   scale=conv_g[:, TAPS - 1, c:c + 1]).then_inc(conv_biased, 1)
                act.wait_ge(group_ready, g * 5 + 5)
                for k in range(4):
                    tick(at(KP + k))
                    for i in (2 * k, 2 * k + 1):
                        full(use(i))
                        act.activation(mix_t[:, i, 0:2 * P], small[:, i % 2, 0:2 * P], ACT.Exp,
                                       bias=per_head_g[:, 0, i:i + 1])
                        act.activation(mix_t[:, i, 2 * P:3 * P], small[:, i % 2, 2 * P:3 * P], ACT.Exp,
                                       bias=per_head_g[:, 1, i:i + 1]).then_inc(small_free_act, 1)
                    if k == 3:
                        act.wait_ge(acc_free_dve, g * 5 + (af_dve_g + 1))
                        act.activation(x_ch[:, :, :], x_ch[:, :, :], ACT.Silu).then_inc(conv_act, 1)
                for k in range(4, 6):
                    tick(at(KP + k))
                for t in range(NT):
                    full(use(8 + t))
                    act.activation(x_tok[:, t, :], small[:, t, :], ACT.Copy).then_inc(small_free_act, 1)
                for k in range(6, 8):
                    tick(at(KP + k))
                done(act, at(2 * KP - 1))
                act.activation(z_act[:, :, :], A[:, :, :], ACT.Silu).then_inc(acc_free_act, 1)
                tick(at(2 * KP))
                for t in range(NT):
                    act.wait_ge(y_gated, g * NT + (t + 1))
                    act.activation(y_skip[:, t, :], z_act[:, t, :], ACT.Square,
                                   accum_out=ss[:, t:t + 1]).then_inc(y_squared, 1)
                for k in range(1, 6):
                    tick(at(2 * KP + k))
                for r in range(2):
                    turn_hi(use(10 + r), r, yt_hi, gain_g, 2 * r)
                for k in range(6, 9):
                    tick(at(2 * KP + k))
                done(act, at(3 * KP - 1))
                half = BANK // 2
                act.activation(gate_a[:, :, :], B[:, :, 0:half], ACT.Sigmoid)
                act.activation(gate_b[:, :, bass.ds(g * half, half)], B[:, :, half:BANK],
                               ACT.Sigmoid).then_inc(acc_free_act, 1)
                for k in range(1, 8):
                    tick(at(3 * KP + k))

            for r in range(2):
                turn_hi(U_late + r, r % 2, act_hi, None, 2 * r)
            for n in range(4 * KP):
                b, k = n // KP, n % KP
                tick(At(n_wout + n))
                if n + 2 < KP:
                    turn_hi(U_late + n + 2, n % 2, act_hi, None, 2 * (n + 2))
                if b == 1 and k < 2:
                    for r in (2 * k, 2 * k + 1):
                        full(U_late + 8 + r)
                        act.activation(keys_t[:, 4 * r:4 * r + 4, :].rearrange("p c k -> p (c k)"),
                                       small[:, r % 2, :], ACT.Copy).then_inc(small_free_act, 1)
                if b and k in X1_AT:
                    x1_turn(2 * (b - 1) + X1_AT.index(k))
            def unit_scores(count, src):
                if not isinstance(count, int) or count:
                    act.wait_ge(unit_ids, count)
                act.activation(sc_u[:, :, :], src, ACT.Copy).then_inc(unit_sc, 1)

            def unit_softmax(count, t):
                act.wait_ge(top_ready, count)
                act.activation(gate[:, t, :], pair_v[:, :], ACT.Exp, bias=g_max[:, 0:1],
                               accum_out=g_sum[:, t:t + 1]).then_inc(gate_exp, 1)

            def query_scores(b):
                for t in range(NT):
                    full(U_late + 20 + NT * b + t)
                    act.activation(sc[t][:, 4 * b:4 * b + 4, :].rearrange("p c k -> p (c k)"),
                                   small[:, t, :], ACT.Copy, scale=rstd[:, t:t + 1]).then_inc(small_free_act, 1)

            for n in range(4 * KP):
                b, k = n // KP, n % KP
                tick(At(n_pq + n))
                if n < 2:
                    x1_turn(6 + n)
                if b and k == SCORES_AT:
                    if b == 1:
                        act.wait_ge(rstd2_ready, 1)
                    query_scores(b - 1)
                    if b == 1:
                        act.wait_ge(small_free_act, sf_act_l + 4 + NT)
                        unit_scores(0, sc[0][:, 0:2, :])
                if n == FIRST_TOP + TOP_TICKS:
                    unit_softmax(1, 0)
                    unit_scores(1, sc[1][:, 0:2, :])
                if k == KP - 1:
                    done(act, At(n_pq + n))
                    act.activation(qp[:, b % 2].rearrange("p c t -> p (c t)"),
                                   (A if b % 2 == 0 else B)[:, :, :].rearrange("p b n -> p (b n)"),
                                   ACT.Copy).then_inc(acc_free_act, 1)
            query_scores(3)
            act.wait_ge(small_free_act, sf_act_l + 4 + 4 * NT)
            act.wait_ge(sc_padded, NT)

            def unit(h, t):
                heads = slice(2 * t, 2 * t + 2) if isinstance(h, int) else bass.ds(h * 2 + 2 * t, 2)
                if not isinstance(h, int) or t:
                    unit_scores(h * NT + (t + 1), sc[1 - t][:, heads, :])
                act.wait_ge(slot_free, h * (NT * UNIT_ROWS) + (t * UNIT_ROWS + PK))
                act.activation(gelu[:, t, :], dots[:, t, :], ACT.Gelu).then_inc(gelued, 1)
                unit_softmax(h * NT + (t + 2), 1 - t)

            for t in range(NT):
                unit(0, t)
            with act.Fori(1, PH) as h:
                for t in range(NT):
                    unit(h, t)

        @block.vector
        def _(dve):
            steps = Steps(dve, dve_step)

            def split(at):
                slot = at.k % RING
                dve.wait_ge(hi_split, at.count(1))
                w = width_of(at)
                dve.tensor_tensor(w_lo[:, slot, :, 0:w], w_raw[:, slot, :, 0:w], w_hi[:, slot, :, 0:w].bitcast(F32),
                                  ALU.subtract).then_inc(lo_split, 1)

            def tick(at):
                if at.per or at.k + AHEAD < n_all:
                    split(at.plus(AHEAD))

            def step(instruction):
                steps.mark(instruction)
                steps.wait()

            def rsqrt(n, width):
                v, y, a, i = rq_v[:, 0:n], rstd[:, 0:n], rq_a[:, 0:n], rq_i[:, 0:n]
                step(dve.tensor_scalar(v, ss[:, 0:n], 1.0 / width, EPS, ALU.mult, ALU.add))
                step(dve.tensor_scalar(i, v.bitcast(I32), 1, None, ALU.logical_shift_right))
                step(dve.tensor_scalar(y.bitcast(I32), i, -1.0, RSQRT_MAGIC, ALU.mult, ALU.add))
                for _ in range(3):
                    step(dve.scalar_tensor_tensor(a, y, -0.5, y, ALU.mult, ALU.mult))
                    step(dve.tensor_tensor(a, a, v, ALU.mult))
                    step(dve.scalar_tensor_tensor(y, a, 1.5, y, ALU.add, ALU.mult))

            RSQRT_STEPS = 3 + 3 * 3

            def conv_taps(acc_sb, ps, biased, first=None):
                dve.wait_ge(conv_biased, biased)
                for back in range(1, TAPS):
                    for c in range(4):
                        if first is None:
                            o = acc_sb[:, c, back:T]
                        else:
                            o = acc_sb[:, bass.ds(first + c, 1), back:T].rearrange("p c t -> p (c t)")
                        ins = dve.scalar_tensor_tensor(o, chan(ps, c)[:, 0:T - back],
                                                       conv_g[:, TAPS - 1 - back, c:c + 1], o, ALU.mult, ALU.add)
                        if back < TAPS - 1:
                            steps.mark(ins)
                    if back < TAPS - 1:
                        steps.wait()
                ins.then_inc(acc_free_dve, 1)

            CONV_STEPS = 4 * (TAPS - 2)

            def turn_lo(count, bank, hi, lo, gain, first):
                dve.wait_ge(turned_hi, count)
                for i in range(2):
                    ins = dve.scalar_tensor_tensor(
                        lo[:, first + i, :], small[:, bank, i * T:(i + 1) * T],
                        1.0 if gain is None else gain[:, first + i:first + i + 1],
                        hi[:, first + i, :].bitcast(F32), ALU.mult, ALU.subtract)
                ins.then_inc(small_free_dve, 1)

            dve.wait_ge(x_landed[0], 16)
            step(dve.tensor_tensor_reduce(x_junk[:, :], x_sb[:, 0, :], x_sb[:, 0, :], 1.0, 0.0, ALU.mult,
                                          ALU.add, ss[:, 0:1]))
            dve.wait_ge(x_squared, 1)
            rsqrt(NT, D)
            dve.sem_inc(x_rstd, 1)
            dve.tensor_scalar(x_sb[:, 0, :], x_sb[:, 0, :], rstd[:, 0:1], None, ALU.mult).then_inc(xn_ready, 1)
            dve.wait_ge(small_full, 1)
            dve.tensor_copy(columns[:, :], small[:, 0, 0:COLS]).then_inc(small_free_dve, 1)
            dve.wait_ge(small_free_dve, 1)
            g1 = columns[:, 5 * CC:5 * CC + KC]
            c_cqg = 5 * CC + KC + XC
            for r in range(2):
                turn_lo(r + 1, (U_turn_x + r) % 2, act_hi, act_lo, g1, 2 * r)
            for n in range(AHEAD):
                split(At(n))
            for n in range(2 * KP + 1):
                tick(At(n))
                if n + 2 < KP:
                    turn_lo(n + 2 + 1, (U_turn_x + n) % 2, act_hi, act_lo, g1, 2 * (n + 2))
                if n == KP - 1:
                    dve.wait_ge(squared, NT)
                    rsqrt(NT, QL)
                    for t in range(NT):
                        ins = dve.tensor_scalar(cqn[:, t, :], A[:, t, 0:QL], rstd[:, t:t + 1], None, ALU.mult)
                    ins.then_inc(acc_free_dve, 1)
                if n - KP in CQ_AT:
                    r = CQ_AT.index(n - KP)
                    turn_lo(8 + r + 1, (U_first + r) % 2, cqt_hi, cqt_lo, columns[:, c_cqg:c_cqg + 4], 2 * r)
                if n == 2 * KP - 1:
                    dve.wait_ge(squared, 2 * NT)
                    rsqrt(NT, KVL)
                    for t in range(NT):
                        dve.tensor_scalar(ckvn[:, t, :], B[:, t, 0:KVL], rstd[:, t:t + 1], None, ALU.mult)
                    for t in range(NT):
                        dve.tensor_copy(kidx2[:, t], B[:, t, KVL:KVL + IDXD].unsqueeze(1).broadcast_to([P, 2, IDXD]))
                    for t in range(NT):
                        ins = dve.tensor_scalar(widx[:, t, :], B[:, t, KVL + IDXD:KVL + IDXD + IDXH],
                                                IDXH ** -0.5 * IDXD ** -0.5, None, ALU.mult)
                    ins.then_inc(acc_free_dve, 1)
                    dve.wait_ge(steps_landed, 48)
                    for t in range(NT):
                        steps.mark(dve.tensor_tensor(sp[:, 0, t * SH:(t + 1) * SH], B[:, t, IN2 - SH:IN2], steps_bc[:, 0, :], ALU.add))
                    steps.wait()
                    dve.tensor_scalar(sp[:, 1, :], sp[:, 0, :], -1.0, None, ALU.mult).then_inc(acc_free_dve, 1)
                    dve.wait_ge(acc_free_dve, 3)
                    dve.tensor_tensor(sp[:, 1, :], sp[:, 1, :], sp[:, 0, :], ALU.min).then_inc(sp_in, 1)
            for b in range(2):
                dve.wait_ge(acc_free_act, b + 1)
                blocks = slice(4 * b, 4 * b + 4)
                dve.tensor_tensor(qi_lo[:, blocks, :].rearrange("p c t -> p (c t)"),
                                  (A, pair_d)[b][:, :, :].rearrange("p b n -> p (b n)"),
                                  qi_hi[:, blocks, :].bitcast(F32).rearrange("p c t -> p (c t)"),
                                  ALU.subtract).then_inc(qi_split, 1)
            turn_lo(11, U_first % 2, ckvt_hi, ckvt_lo, columns[:, c_cqg + 4:c_cqg + 6], 0)
            dve.wait_ge(small_full, U_first + 4)
            step(dve.tensor_copy(ki_hi[:, :], small[:, (U_first + 3) % 2, 0:T]))
            dve.tensor_tensor(ki_lo[:, :], small[:, (U_first + 3) % 2, 0:T], ki_hi[:, :].bitcast(F32),
                              ALU.subtract).then_inc(small_free_dve, 1)

            def softplus(h):
                if h == 0:
                    dve.wait_ge(sp_exp, 2)
                    step(dve.tensor_scalar(sp[:, 3, :], sp[:, 2, :], 2.0, None, ALU.add))
                    step(dve.reciprocal(sp[:, 3, :], sp[:, 3, :]))
                    step(dve.tensor_tensor(sp[:, 3, :], sp[:, 3, :], sp[:, 2, :], ALU.mult))
                if h == 1:
                    step(dve.tensor_tensor(sp[:, 4, :], sp[:, 3, :], sp[:, 3, :], ALU.mult))
                    step(dve.tensor_scalar(sp[:, 5, :], sp[:, 4, :], 1.0 / 17, None, ALU.mult))
                if 2 <= h <= 8:
                    step(dve.scalar_tensor_tensor(sp[:, 5, :], sp[:, 5, :], 1.0 / (19 - 2 * h), sp[:, 4, :],
                                                  ALU.add, ALU.mult))
                if h == 9:
                    step(dve.scalar_tensor_tensor(sp[:, 5, :], sp[:, 5, :], 1.0, sp[:, 3, :], ALU.add, ALU.mult))
                    step(dve.tensor_scalar(sp[:, 5, :], sp[:, 5, :], 2.0, None, ALU.mult))
                    step(dve.tensor_scalar(sp[:, 0, :], sp[:, 0, :], 0.0, None, ALU.max))
                if h == 10:
                    dt = per_head[:, 2:4, :].rearrange("p t h -> p (t h)")
                    step(dve.tensor_tensor(dt, sp[:, 5, :], sp[:, 0, :], ALU.add))
                    for t in range(NT):
                        ins = dve.scalar_tensor_tensor(sp[:, 6, t * SH:(t + 1) * SH], sp[:, 7, 0:SH], -1.0,
                                                       per_head[:, 2 + t, :], ALU.mult, ALU.mult)
                    ins.then_inc(da_ready, 1)

            for h in range(IDXH):
                dve.wait_ge(small_free_act, h + 1)
                for t in range(NT):
                    w = widx[:, t, h:h + 1]
                    if h == 0:
                        ins = dve.tensor_scalar(score[:, t, :], relu[:, 0, t, :], w, None, ALU.mult)
                    else:
                        if t == 0:
                            dve.wait_ge(relu_used, h)
                        ins = dve.scalar_tensor_tensor(score[:, t, :], relu[:, h % 2, t, :], w, score[:, t, :],
                                                       ALU.mult, ALU.add)
                ins.then_inc(relu_used, 1)
                softplus(h)
                if h in (11, 12, 13):
                    tick(At(n_idx + h - 10))
            dve.wait_ge(da_hi, 1)
            dve.tensor_tensor(da_split[:, 2:4, :], sp[:, 6, :].rearrange("p (t h) -> p t h", t=NT),
                              da_split[:, 0:2, :].bitcast(F32), ALU.subtract).then_inc(da_lo, 1)
            dve.wait_ge(small_full, U_cum + 1)
            dve.tensor_scalar(per_head[:, 0:2, :].rearrange("p t h -> p (t h)"), small[:, U_cum % 2, 0:NT * SH], -1.0, None,
                              ALU.mult).then_inc(small_free_dve, 1)
            dve.wait_ge(relu_used, IDXH)
            dve.wait_ge(consts, N_CONSTS)
            step(dve.tensor_tensor(score[:, :, :], score[:, :, :], causal[:, :, :], ALU.min))
            for t in range(NT):
                for _ in range(TOPK // 8):
                    seen = score[:, t, 0:(t + 1) * P]
                    step(dve.max(m8[:, :], seen))
                    step(dve.match_replace(seen, m8[:, :], seen, TAKEN))
                tick(At(n_attn + t))
            step(dve.tensor_scalar(keep[:, 0:P], score[:, 0, 0:P], -FAR * 1.1, NEG, ALU.is_gt, ALU.mult))
            step(dve.tensor_scalar(keep[:, P:3 * P], score[:, 1, :], -FAR * 1.1, NEG, ALU.is_gt, ALU.mult))
            step(dve.tensor_tensor(keep[:, :], keep[:, :], keep_c[:, :], ALU.min))

            with dve.Fori(0, J) as j:
                def at(k):
                    return At(n_attn + k, j, J_P)

                def use(k):
                    return j * J_U + (U_attn + k)

                steps.enter(j, RSQRT_STEPS + 1 + 4 * 2 + 4 + CONV_STEPS)
                dve.wait_ge(squared, j * 5 + (2 * NT + 1))
                dve.tensor_reduce(ss[:, 0:8], sq[:, :, :], AX.X, ALU.add).then_inc(sq_used, 1)
                tick(at(2))
                tick(at(3))
                dve.wait_ge(squared, j * 5 + (2 * NT + 5))
                dve.tensor_reduce(ss[:, 8:16], sq[:, :, :], AX.X, ALU.add).then_inc(sq_used, 1)
                dve.wait_ge(sq_used, j * 2 + 2)
                rsqrt(16, HD)
                dve.wait_ge(acc_free_act, j * 3 + (af_act_j + 3))
                for t in range(NT):
                    dve.tensor_tensor(kv_raw[:, t, :, 0:HD], kv_raw[:, t, :, 0:HD],
                                      rstd[:, 8 + 4 * t:12 + 4 * t].unsqueeze(2).broadcast_to([P, 4, HD]),
                                      ALU.mult).then_inc(qn_ready, 1)
                steps.mark(dve.tensor_scalar(rstd[:, 0:8], rstd[:, 0:8], HD ** -0.5, None, ALU.mult))
                for k in range(4, 8):
                    tick(at(k))
                steps.wait()

                def copy_turned(h):
                    dve.wait_ge(small_full, use(8 + h) + 1)
                    dve.tensor_copy(prob_t[:, h % 2, :], small[:, h % 2, 0:3 * P]).then_inc(small_free_dve, 1)

                for pair in range(2):
                    for h in (2 * pair, 2 * pair + 1):
                        dve.wait_ge(small_full, use(4 + h) + 1)
                        for t, (a, b) in enumerate(((0, P), (P, 3 * P))):
                            ins = dve.scalar_tensor_tensor(prob[:, h, a:b], small[:, h % 2, a:b],
                                                           rstd[:, 4 * t + h:4 * t + h + 1], keep[:, a:b],
                                                           ALU.mult, ALU.add)
                        ins.then_inc(small_free_dve, 1)
                        dve.wait_ge(small_free_dve, j * J_DVE + (sf_dve_j + h + 1))
                        for t, (a, b) in enumerate(((0, P), (P, 3 * P))):
                            steps.mark(dve.tensor_reduce(row_max[:, h, t:t + 1], prob[:, h, a:b], AX.X, ALU.max))
                        steps.wait()
                        dve.tensor_scalar(row_max[:, h, :], row_max[:, h, :], -1.0, None, ALU.mult).then_inc(masked, 1)
                    tick(at(8 + pair))
                    for h in ((0, 1) if pair else ()):
                        copy_turned(h)
                    for h in (2 * pair, 2 * pair + 1):
                        dve.wait_ge(exped, j * 8 + (2 * h + 2))
                        step(dve.reciprocal(row_inv[:, h, :], row_sum[:, h, :]))
                        for t, (a, b) in enumerate(((0, P), (P, 3 * P))):
                            ins = dve.tensor_scalar(prob[:, h, a:b], prob[:, h, a:b], row_inv[:, h, t:t + 1], None,
                                                    ALU.mult)
                        ins.then_inc(probs, 1)
                tick(at(10))
                tick(at(11))
                for h in (2, 3):
                    copy_turned(h)
                for r in range(2):
                    dve.wait_ge(turned_hi, j * 2 + (T_j + r + 1))
                    heads = bass.ds(j * 4 + 2 * r, 2)
                    dve.tensor_tensor(attn_lo[:, heads, :], A[:, r, :].rearrange("p (h t) -> p h t", h=2),
                                      attn_hi[:, heads, :].bitcast(F32), ALU.subtract).then_inc(acc_free_dve, 1)
                conv_taps(bc_t, pair_d, j * 4 + 4, j * 4)
                tick(at(J_P))
                tick(at(J_P + 1))
                steps.leave(J)

            for k in range(2, 4 * KP):
                tick(At(n_ya + k))

            with dve.Fori(0, SG) as g:
                def at(k):
                    return At(n_ssm + k, g, G_P)

                steps.enter(g, CONV_STEPS + RSQRT_STEPS)
                for k in range(KP):
                    tick(at(k))
                conv_taps(x_ch, B, g * 4 + (4 * J + 4))
                dve.wait_ge(cb_full, g + 1)
                dve.wait_ge(group_ready, g * 5 + 5)
                for k in range(4):
                    tick(at(KP + k))
                    for i in (2 * k, 2 * k + 1):
                        dve.wait_ge(small_free_act, g * G_ACT + (sf_act_g + i + 1))
                        dve.scalar_tensor_tensor(mix_t[:, i, 0:2 * P], mix_t[:, i, 0:2 * P], per_head_g[:, 2, i:i + 1],
                                                 pair_d[:, 0, 0:2 * P], ALU.mult, ALU.mult)
                        dve.scalar_tensor_tensor(mix_t[:, i, 2 * P:3 * P], mix_t[:, i, 2 * P:3 * P],
                                                 per_head_g[:, 3, i:i + 1], pair_d[:, 0, 2 * P:3 * P],
                                                 ALU.mult, ALU.mult).then_inc(mixed_t, 1)
                for k in range(4, 9):
                    tick(at(KP + k))
                dve.wait_ge(y_full, g + 1)
                dve.wait_ge(acc_free_act, g * 2 + (af_act_g + 1))
                for t in range(NT):
                    dve.wait_ge(skip_ready, g * NT + (t + 1))
                    dve.tensor_tensor(y_skip[:, t, :], y_skip[:, t, :], pair_d[:, t, :], ALU.add).then_inc(y_taken, 1)
                for t in range(NT):
                    dve.wait_ge(y_taken, g * NT + (t + 1))
                    dve.tensor_tensor(z_act[:, t, :], z_act[:, t, :], y_skip[:, t, :], ALU.mult).then_inc(y_gated, 1)
                for k in range(1, 3):
                    tick(at(2 * KP + k))
                dve.wait_ge(y_squared, g * NT + NT)
                rsqrt(NT, INNER // SG)
                for t in range(NT):
                    dve.tensor_scalar(z_act[:, t, :], z_act[:, t, :], rstd[:, t:t + 1], None,
                                      ALU.mult).then_inc(yn_ready, 1)
                for k in range(3, 6):
                    tick(at(2 * KP + k))
                for r in range(2):
                    turn_lo(g * 2 + (T_g + r + 1), r, yt_hi, yt_lo, gain_g, 2 * r)
                for k in range(6, 10):
                    tick(at(2 * KP + k))
                dve.wait_ge(yb_ready, 1)
                for d in range(4):
                    tick(at(3 * KP + 2 * d + 2) if d < 3 else at(G_P - 1))
                    done(dve, at(3 * KP + 2 * d + 1))
                    dve.wait_ge(acc_free_dve, g * 5 + (af_dve_g + 1 + d - 1 if d else af_dve_g))
                    ps = (A, B, A, pair_d)[d]
                    dve.tensor_tensor(yb[:, :, d * BANK:(d + 1) * BANK], yb[:, :, d * BANK:(d + 1) * BANK],
                                      ps[:, :, :], ALU.add).then_inc(acc_free_dve, 1)
                    if d < 2:
                        tick(at(3 * KP + 2 * d + 3))
                steps.leave(SG)

            def x1_turn(r):
                turn_lo(T_l + 8 + r + 1, r % 2, q_act_hi, q_act_lo, columns[:, COLS - KC:COLS], 2 * r)

            for r in range(2):
                turn_lo(T_l + r + 1, r % 2, act_hi, act_lo, None, 2 * r)
            for n in range(4 * KP):
                b, k = n // KP, n % KP
                tick(At(n_wout + n))
                if n + 2 < KP:
                    turn_lo(T_l + n + 2 + 1, n % 2, act_hi, act_lo, None, 2 * (n + 2))
                if b and k in X1_AT:
                    x1_turn(2 * (b - 1) + X1_AT.index(k))
                if k == KP - 1:
                    done(dve, At(n_wout + n))
                    if b == 0:
                        dve.wait_ge(late_landed[0], 16 * NT)
                    cols = slice(b * BANK, (b + 1) * BANK)
                    dve.tensor_tensor(x1[:, :, cols], x1[:, :, cols], (A, B)[b % 2][:, :, :],
                                      ALU.add).then_inc(acc_free_dve, 1)

            def top_experts(count, t, between=None):
                def wait():
                    steps.wait_apart(dve_passed)

                flat = cand[:, :, :].rearrange("p i j -> p (i j)")

                def best16(vals, idxs, tables):
                    for k in range(2):
                        e = slice(8 * k, 8 * k + 8)
                        for v, tb in zip(vals, tables):
                            steps.mark(dve.max(v[:, e], tb))
                        wait()
                        for v, ix, tb in zip(vals, idxs, tables):
                            steps.mark(dve.max_index(ix[:, e], v[:, e], tb))
                            if k == 0:
                                steps.mark(dve.match_replace(tb, v[:, e], tb, TAKEN))
                        wait()

                dve.wait_ge(unit_sc, count)
                if not isinstance(count, int) or count > 1:
                    dve.wait_ge(gate_exp, count - 1)
                steps.mark(dve.tensor_copy(part[:, 0, :], iota16[:, :]))
                wait()
                best16([top_v[:, c, :] for c in range(2)], [top_i[:, c, :] for c in range(2)],
                       [sc_u[:, c, :] for c in range(2)])
                if between:
                    between()
                steps.mark(dve.tensor_copy(top_f[:, :, :], top_i[:, :, :]))
                steps.mark(dve.tensor_tensor(cand[:, :, :], top_v[:, 0, :].unsqueeze(2).broadcast_to([P, PK, PK]),
                                             top_v[:, 1, :].unsqueeze(1).broadcast_to([P, PK, PK]), ALU.add))
                wait()
                best16([pair_v], [pair_i], [flat])
                dve.tensor_scalar(g_max[:, 0:1], pair_v[:, 0:1], -1.0, None, ALU.mult).then_inc(top_ready, 1)
                if between:
                    between()
                steps.mark(dve.tensor_scalar(pair_hl[:, 0, :], pair_i[:, :], 4, None, ALU.logical_shift_right))
                steps.mark(dve.tensor_scalar(pair_hl[:, 1, :], pair_i[:, :], PK - 1, None, ALU.bitwise_and))
                steps.wait()
                step(dve.tensor_copy(pair_f[:, :, :], pair_hl[:, :, :]))
                picks = (pick, cand)
                for c in range(2):
                    steps.mark(dve.tensor_tensor(picks[c][:, :, :], pair_f[:, c, :].unsqueeze(2).broadcast_to([P, PK, PK]),
                                                 iota16[:, :].unsqueeze(1).broadcast_to([P, PK, PK]), ALU.is_equal))
                steps.wait()
                for c in range(2):
                    steps.mark(dve.tensor_tensor(picks[c][:, :, :], picks[c][:, :, :],
                                                 top_f[:, c, :].unsqueeze(1).broadcast_to([P, PK, PK]), ALU.mult))
                steps.wait()
                for c in range(2):
                    steps.mark(dve.tensor_reduce(part[:, c, :], picks[c][:, :, :], AX.X, ALU.add))
                steps.wait()
                dve.scalar_tensor_tensor(eid[:, t, :], part[:, 0, :], float(NK), part[:, 1, :], ALU.mult,
                                         ALU.add).then_inc(unit_ids, 1)

            TOP_STEPS = 1 + (2 + 4 + 2 + 2) + 2 + (1 + 2 + 1 + 1) + 2 + 1 + 2 + 2 + 2
            def unit(h, t, early, between=None):
                def landed(i):
                    slot = slot_of(i, early)
                    if early:
                        dve.wait_ge(gathered[slot], (i // EARLY + 1) * 16)
                    else:
                        per = NT * UNIT_ROWS // GATHERS * 16
                        first = NT * UNIT_ROWS // EARLY * 16 if slot < EARLY else 0
                        dve.wait_ge(gathered[slot], h * per + (first - per + (i // GATHERS + 1) * 16))
                    return slots[:, slot, :]

                dotted = [0]

                def some_dots():
                    for k in range(dotted[0], dotted[0] + PK // 4):
                        slot = landed(t * UNIT_ROWS + k)
                        dve.tensor_tensor_reduce(slot, slot, h2[:, t, :], 1.0, 0.0, ALU.mult, ALU.add,
                                                 dots[:, t, k:k + 1]).then_inc(slot_free, 1)
                        if between:
                            between(k)
                    dotted[0] += PK // 4

                some_dots()
                top_experts(h * NT + (t + 2), 1 - t, some_dots)
                some_dots()
                dve.wait_ge(gate_exp, h * NT + (t + 1))
                step(dve.reciprocal(g_inv[:, 0:1], g_sum[:, t:t + 1]))
                dve.wait_ge(gelued, h * NT + (t + 1))
                dve.scalar_tensor_tensor(share[:, t, :], gelu[:, t, :], g_inv[:, 0:1], gate[:, t, :], ALU.mult,
                                         ALU.mult).then_inc(shared, 1)
                dve.wait_ge(shared, h * NT + (t + 1))
                for k in range(PK):
                    i = t * UNIT_ROWS + PK + k
                    slot = landed(i)
                    dve.wait_ge(slot_free, h * (NT * UNIT_ROWS) + i)
                    dve.scalar_tensor_tensor(x1[:, t, :], slot, share[:, t, k:k + 1],
                                             x1[:, t, :], ALU.mult, ALU.add).then_inc(slot_free, 1)

            def next_tick():
                if ticked[0] < 4 * KP:
                    tick(At(n_pq + ticked[0]))
                    ticked[0] += 1

            ticked = [0]
            for n in range(FIRST_TOP + 1):
                next_tick()
                if n < 2:
                    x1_turn(6 + n)
                if n == 2:
                    dve.wait_ge(x1_squared, 4 * NT)
                    step(dve.tensor_reduce(ss[:, 0:NT], ss[:, 8:16].rearrange("p (t d) -> p t d", d=4), AX.X, ALU.add))
                    rsqrt(NT, D)
                    dve.sem_inc(rstd2_ready, 1)
                    dve.wait_ge(late_landed[2], 16)
                    dve.wait_ge(small_free_act, sf_act_l + 4)
                    dve.wait_ge(acc_free_dve, af_dve_l + 4)
                if 3 <= n < 3 + NT:
                    t = n - 3
                    dve.scalar_tensor_tensor(h2[:, t, :], x1[:, t, :], rstd[:, t:t + 1], gain2[:, :],
                                             ALU.mult, ALU.mult).then_inc(h2_ready, 1)
            top_experts(1, 0, next_tick)
            next_tick()
            dve.wait_ge(h2_ready, NT)
            for t in range(NT):
                unit(0, t, True, (lambda k: (next_tick(), next_tick() if k % 4 == 3 else None)) if t == 0 else None)
            assert ticked[0] == 4 * KP
            with dve.Fori(1, PH) as h:
                steps.enter(h, NT * (TOP_STEPS + 1), 1)
                for t in range(NT):
                    unit(h, t, False)
                steps.leave(PH - 1)

        @block.tensor
        def _(pe):
            def piece(at, width, acc_out, hi, lo, kc, first, last, channels):
                slot = at.k % RING
                pe.wait_ge(lo_split, at.count(1))
                for i in range(PIECE_KC):
                    start, stop = first and i == 0, last and i == PIECE_KC - 1
                    if channels:
                        for c in range(4):
                            o = chan(acc_out, c)
                            wh = w_hi[:, slot, i, c * P:(c + 1) * P]
                            wl = w_lo[:, slot, i, c * P:(c + 1) * P]
                            ah, al = hi[:, kc + i, :], lo[:, kc + i, :]
                            pe.matmul(o, wh, ah, start=start and c % 2 == 0, stop=False, skip_group_check=True)
                            pe.matmul(o, wh, al, start=False, stop=False, skip_group_check=True)
                            ins = pe.matmul(o, wl, ah, start=False, stop=stop, skip_group_check=True)
                    else:
                        for t in range(NT):
                            o = acc_out[:, t, 0:width]
                            wh, wl = w_hi[:, slot, i, 0:width], w_lo[:, slot, i, 0:width]
                            ah, al = hi[:, kc + i, t * P:(t + 1) * P], lo[:, kc + i, t * P:(t + 1) * P]
                            pe.matmul(o, ah, wh, start=start, stop=False)
                            pe.matmul(o, ah, wl, start=False, stop=False)
                            ins = pe.matmul(o, al, wh, start=False, stop=stop)
                ins.then_inc(w_used, 1)

            def pieces(at, which, width, acc_out, channels=False):
                for k in which:
                    piece(at.plus(k), width, acc_out, act_hi, act_lo, PIECE_KC * k, k == 0, k == KP - 1, channels)

            def transpose_to(out, in_, n=P):
                return pe.transpose(out, in_, ident[0:n, 0:n])

            def turn(bank, src, first):
                for i in range(2):
                    for t in range(NT):
                        ins = transpose_to(small[:, bank, i * T + t * P:i * T + (t + 1) * P],
                                           src[:, t, (first + i) * P:(first + i + 1) * P])
                ins.then_inc(small_full, 1)

            pe.wait_ge(rows_landed, 10 * 16)
            pe.wait_ge(consts, N_CONSTS)
            transpose_to(small[:, 0, 0:2 * CC], rows[0:2 * CC, 0, :], 2 * CC)
            transpose_to(small[:, 0, 2 * CC:4 * CC], rows[0:2 * CC, 1, :], 2 * CC)
            n_vec = COLS - 4 * CC
            transpose_to(small[:, 0, 4 * CC:COLS], rows[0:n_vec, 2, :], n_vec).then_inc(small_full, 1)
            pe.wait_ge(xn_ready, NT)

            def turn_x(r):
                if r >= 1:
                    pe.wait_ge(small_free_dve, r)
                turn((U_turn_x + r) % 2, x_sb, 2 * r)

            turn_x(0)
            turn_x(1)
            for k in range(KP):
                pe.wait_ge(small_free_dve, U_turn_x + k + 1)
                pieces(At(0), range(k, k + 1), QL, A)
                if k + 2 < KP:
                    turn_x(k + 2)
            for k in range(KP):
                pieces(At(KP), range(k, k + 1), IN2, B)
                if k in CQ_AT:
                    if k == CQ_AT[0]:
                        pe.wait_ge(acc_free_dve, 1)
                    r = CQ_AT.index(k)
                    turn((U_first + r) % 2, cqn, 2 * r)
            pe.wait_ge(small_free_dve, S0_dve + 2)
            for b, o in ((0, A), (1, pair_d)):
                for k in range(2):
                    piece(At(n_idx + 2 * b + k), BANK, o, cqt_hi, cqt_lo, 2 * k, k == 0, k == 1, True)
            pe.wait_ge(acc_free_dve, 3)
            turn((U_first + 2) % 2, ckvn, 0)
            for t in range(NT):
                ins = transpose_to(small[:, (U_first + 3) % 2, t * P:(t + 1) * P],
                                   kidx2[:, t].rearrange("p a d -> p (a d)"))
            ins.then_inc(small_full, 1)
            pe.wait_ge(small_free_dve, S0_dve + 4)
            pe.wait_ge(qi_split, 2)
            for h in range(IDXH):
                half = slice(IDXD * (h % 2), IDXD * (h % 2) + IDXD)
                if h >= 2:
                    pe.wait_ge(small_free_act, h - 1)
                for t in range(NT):
                    o = small[:, (U_idx + h) % 2, t * T:(t + 1) * T]
                    q_hi = qi_hi[half, h // 2, t * P:(t + 1) * P]
                    pe.matmul(o, q_hi, ki_hi[half, :], start=True, stop=False)
                    pe.matmul(o, q_hi, ki_lo[half, :], start=False, stop=False)
                    ins = pe.matmul(o, qi_lo[half, h // 2, t * P:(t + 1) * P], ki_hi[half, :], start=False, stop=True)
                ins.then_inc(small_full, 1)
            pe.wait_ge(small_free_act, IDXH)
            pe.wait_ge(da_lo, 1)
            cum = small[:, U_cum % 2, 0:NT * SH].rearrange("p (t h) -> p t h", t=NT)
            pe.matmul(cum[:, 0, :], cum_rhs0[:, 0, :], da_split[:, 0, :], start=True, stop=False)
            pe.matmul(cum[:, 0, :], cum_rhs0[:, 0, :], da_split[:, 2, :], start=False, stop=True)
            pe.matmul(cum[:, 1, :], cum_rhs0[:, 1, :], da_split[:, 0, :], start=True, stop=False)
            pe.matmul(cum[:, 1, :], cum_rhs0[:, 1, :], da_split[:, 2, :], start=False, stop=False)
            pe.matmul(cum[:, 1, :], cum_rhs0[:, 0, :], da_split[:, 1, :], start=False, stop=False)
            pe.matmul(cum[:, 1, :], cum_rhs0[:, 0, :], da_split[:, 3, :], start=False, stop=True).then_inc(small_full, 1)

            with pe.Fori(0, J) as j:
                def at(k):
                    return At(n_attn + k, j, J_P)

                def act_free(n):
                    pe.wait_ge(small_free_act, j * J_ACT + (sf_act_j + n))

                def dve_free(n):
                    pe.wait_ge(small_free_dve, j * J_DVE + (sf_dve_j + n))

                def bc(first, n=1):
                    pieces(at(4), range(first, first + n), BANK, pair_d, True)

                def turn_pair(src, k):
                    for i in range(2):
                        for t in range(NT):
                            ins = transpose_to(small[:, k % 2, i * T + t * P:i * T + (t + 1) * P],
                                               src[:, t, 2 * (k % 2) + i, 0:HD])
                    ins.then_inc(small_full, 1)

                def scores(h):
                    o = small[:, h % 2, :]
                    pe.matmul(o[:, 0:P], q_t[:, h, 0:P], k_t[:, h, 0:P], start=True, stop=True)
                    pe.matmul(o[:, P:3 * P], q_t[:, h, P:2 * P], k_t[:, h, :], start=True, stop=True).then_inc(small_full, 1)

                def turn_probs(h):
                    pe.wait_ge(probs, j * 4 + (h + 1))
                    dve_free(3 + h)
                    for b in range(3):
                        ins = transpose_to(small[:, h % 2, b * P:(b + 1) * P], prob[:, h, b * P:(b + 1) * P])
                    ins.then_inc(small_full, 1)

                def weigh(r):
                    for i in range(2):
                        h = 2 * r + i
                        o = A[:, r, i * T:(i + 1) * T]
                        pe.matmul(o, kv_raw[:, 0, h, HD:2 * HD], prob_t[:, i, 0:2 * P], start=True, stop=False)
                        ins = pe.matmul(o[:, P:2 * P], kv_raw[:, 1, h, HD:2 * HD], prob_t[:, i, 2 * P:3 * P],
                                        start=False, stop=True)
                    ins.then_inc(heads_full, 1)

                pe.wait_ge(acc_free_act, j * 3 + af_act_j)
                for k in range(2):
                    piece(at(k), BANK, B, cqt_hi, cqt_lo, 2 * k, k == 0, k == 1, False)
                pe.wait_ge(acc_free_dve, j * J_AD + (af_dve_j - 1))
                piece(at(2), BANK, A, ckvt_hi, ckvt_lo, 0, True, True, False)
                pe.wait_ge(acc_free_act, j * 3 + (af_act_j + 1))
                piece(at(3), BANK, B, ckvt_hi, ckvt_lo, 0, True, True, False)
                dve_free(0)
                act_free(0)
                turn_pair(q_raw, 0)
                turn_pair(q_raw, 1)
                pe.wait_ge(acc_free_dve, j * J_AD + af_dve_j)
                bc(0)
                bc(1, 2)
                pe.wait_ge(qn_ready, j * NT + NT)
                act_free(1)
                turn_pair(kv_raw, 2)
                act_free(2)
                turn_pair(kv_raw, 3)
                bc(3)
                act_free(4)
                scores(0)
                scores(1)
                bc(4)
                dve_free(1)
                scores(2)
                dve_free(2)
                scores(3)
                bc(5)
                turn_probs(0)
                turn_probs(1)
                bc(6)
                dve_free(6)
                weigh(0)
                turn_probs(2)
                turn_probs(3)
                bc(7)
                dve_free(8)
                weigh(1)

            pe.wait_ge(small_free_dve, sf_dve_g)
            with pe.Fori(0, 2) as d:
                for b, o in ((0, B), (1, A)):
                    pe.wait_ge(acc_free_act, d * 2 + af_act_y)
                    if b:
                        pe.wait_ge(acc_free_dve, af_dve_y)
                    for k in range(KP):
                        piece(At(n_ya + b * KP + k, d, 2 * KP), BANK, o, attn_hi, attn_lo, 2 * k, k == 0, k == KP - 1, False)

            with pe.Fori(0, SG) as g:
                def at(k):
                    return At(n_ssm + k, g, G_P)

                def act_free(n):
                    pe.wait_ge(small_free_act, g * G_ACT + (sf_act_g + n))

                pe.wait_ge(acc_free_act, g * 2 + af_act_g)
                pe.wait_ge(acc_free_dve, g * 5 + (af_dve_g - 2))
                pieces(at(0), range(KP), BANK, B, True)
                pe.wait_ge(group_ready, g * 5 + 5)
                pe.wait_ge(acc_free_dve, g * 5 + af_dve_g)
                pe.matmul(pair_d[:, 0, 0:2 * P], bc_g[:, 0, 0:P], bc_g[:, 1, :], start=True, stop=True)
                pe.matmul(pair_d[:, 0, 2 * P:3 * P], bc_g[:, 0, P:2 * P], bc_g[:, 1, P:2 * P], start=True,
                          stop=True).then_inc(cb_full, 1)
                pe.wait_ge(small_free_dve, g * G_DVE + sf_dve_g)
                for k in range(KP):
                    pieces(at(KP), range(k, k + 1), BANK, A)
                    for i in ((2 * k, 2 * k + 1) if k < 4 else ()):
                        if i >= 2:
                            act_free(i - 1)
                        o = small[:, i % 2, 0:3 * P]
                        for part_, (ta, tb) in enumerate(((0, 1), (2, 3))):
                            pe.matmul(o, da_g[:, ta, i:i + 1].broadcast_to([P, P]),
                                      cum_rhs0[:, :, :].rearrange("p a b -> p (a b)"), start=part_ == 0, stop=False)
                            pe.matmul(o[:, P:3 * P], da_g[:, tb, i:i + 1].broadcast_to([P, P]),
                                      cum_rhs1[:, :, :].rearrange("p a b -> p (a b)"), start=False, stop=False)
                        pe.matmul(o[:, 0:P], ident_r[:, :], future_r[:, :], start=False, stop=False)
                        pe.matmul(o[:, 2 * P:3 * P], ident_r[:, :], future_r[:, :], start=False,
                                  stop=True).then_inc(small_full, 1)
                    if k == 5:
                        pe.wait_ge(conv_act, g + (4 + 1))
                        for t in range(NT):
                            act_free(7 + t)
                            for c in range(4):
                                ins = transpose_to(small[:, t, c * P:(c + 1) * P], x_ch[:, c, t * P:(t + 1) * P])
                            ins.then_inc(small_full, 1)
                pe.wait_ge(mixed_t, g * GH + GH)
                act_free(10)
                for i in range(GH):
                    cols = slice(i * SHD, (i + 1) * SHD)
                    pe.matmul(pair_d[:, 0, cols], mix_t[:, i, 0:P], x_tok[:, 0, cols], start=True, stop=True)
                    pe.matmul(pair_d[:, 1, cols], mix_t[:, i, P:2 * P], x_tok[:, 0, cols], start=True, stop=False)
                    ins = pe.matmul(pair_d[:, 1, cols], mix_t[:, i, 2 * P:3 * P], x_tok[:, 1, cols], start=False, stop=True)
                ins.then_inc(y_full, 1)
                pe.wait_ge(acc_free_dve, g * 5 + (af_dve_g + 1))
                pieces(at(2 * KP), range(0, 6), BANK, B)
                pe.wait_ge(yn_ready, g * NT + NT)
                for r in range(2):
                    turn(r, z_act, 2 * r)
                pieces(at(2 * KP), range(6, 8), BANK, B)
                pe.wait_ge(small_free_dve, g * G_DVE + (sf_dve_g + 2))
                for d, o in enumerate((A, B, A, pair_d)):
                    if d < 2:
                        pe.wait_ge(acc_free_act, g * 2 + (af_act_g + 1 + d))
                    if d == 2:
                        pe.wait_ge(acc_free_dve, g * 5 + (af_dve_g + 2))
                    for k in range(2):
                        piece(at(3 * KP + 2 * d + k), BANK, o, yt_hi, yt_lo, 2 * k, k == 0, k == 1, False)

            def turn_merged(r):
                pe.wait_ge(mixed, r // 2 + 1)
                if r >= 2:
                    pe.wait_ge(small_free_dve, sf_dve_l + r - 1)
                turn(r % 2, ya, 2 * r)

            def turn_keys(r):
                if r >= 2:
                    pe.wait_ge(small_free_act, sf_act_l + r - 1)
                for c in range(4):
                    ins = transpose_to(small[:, r % 2, c * P:(c + 1) * P], keys[:, 4 * r + c, :])
                ins.then_inc(small_full, 1)

            def turn_x1(r):
                if r % 2 == 0:
                    pe.wait_ge(acc_free_dve, af_dve_l + r // 2 + 1)
                if r >= 2:
                    pe.wait_ge(small_free_dve, sf_dve_l + 8 + r - 1)
                turn(r % 2, x1, 2 * r)

            turn_merged(0)
            turn_merged(1)
            for n in range(4 * KP):
                b, k = n // KP, n % KP
                if b == 0:
                    pe.wait_ge(small_free_dve, sf_dve_l + k + 1)
                if k == 0:
                    pe.wait_ge(acc_free_dve, af_dve_l + max(b - 1, 0))
                pieces(At(n_wout + b * KP), range(k, k + 1), BANK, (A, B)[b % 2])
                if n + 2 < KP:
                    turn_merged(n + 2)
                if b == 1 and k < 2:
                    if k == 0:
                        pe.wait_ge(late_landed[1], 16)
                    turn_keys(2 * k)
                    turn_keys(2 * k + 1)
                if b and k in X1_AT:
                    if n == KP + X1_AT[0]:
                        pe.wait_ge(small_free_act, sf_act_l + 4)
                    turn_x1(2 * (b - 1) + X1_AT.index(k))

            def key_scores(b):
                pe.wait_ge(acc_free_act, af_act_l + b + 1)
                for t in range(NT):
                    if b:
                        pe.wait_ge(small_free_act, sf_act_l + 4 + NT * (b - 1) + t + 1)
                    for c in range(4):
                        ins = pe.matmul(small[:, t, c * NK:(c + 1) * NK], qp[:, b % 2, c, t * P:(t + 1) * P],
                                        keys_t[:, 4 * b + c, :], start=True, stop=True)
                    ins.then_inc(small_full, 1)

            for n in range(4 * KP):
                b, k = n // KP, n % KP
                if n == 0:
                    pe.wait_ge(acc_free_dve, af_dve_l + 3)
                    pe.wait_ge(small_free_dve, sf_dve_l + 8 + 6)
                if n in (6, 7):
                    pe.wait_ge(small_free_dve, sf_dve_l + 8 + n + 1)
                if k == 0 and b:
                    pe.wait_ge(acc_free_dve, af_dve_l + 4)
                if k == 0 and b >= 2:
                    pe.wait_ge(acc_free_act, af_act_l + b - 1)
                piece(At(n_pq + n), BANK, (A, B)[b % 2], q_act_hi, q_act_lo, PIECE_KC * k, k == 0, k == KP - 1, True)
                if n < 2:
                    turn_x1(6 + n)
                if k == SCORES_AT and b:
                    key_scores(b - 1)
            key_scores(3)


_INS = ["x", "g_norm1", "w_in", "g_cq", "g_ckv", "w_uq", "w_ukv", "g_qn", "g_kn", "w_iq", "w_o_attn",
        "conv_w", "conv_b", "dt_bias", "a_log", "d_skip", "g_ssm", "w_o_ssm", "w_out",
        "g_norm2", "w_peer_q", "peer_keys", "peer_u", "peer_v"]
_OUTS = [((1, 256, 2048), "float32")]


def kernel(**inputs):
    import numpy as _np
    import concourse.bacc as _bacc
    from concourse import mybir as _mybir
    from concourse.bass_utils import run_bass_kernel_spmd as _run

    nc = _bacc.Bacc("TRN2", target_bir_lowering=False, num_devices=1)
    arrays, args = {}, []
    for name in _INS:
        a = _np.ascontiguousarray(inputs[name])
        arrays[f"in_{name}_dram"] = a
        args.append(nc.dram_tensor(f"in_{name}_dram", a.shape, _mybir.dt.from_np(a.dtype), kind="ExternalInput").ap())
    for i, (shape, dtype) in enumerate(_OUTS):
        dt = _mybir.dt.from_np(_np.dtype(dtype))
        args.append(nc.dram_tensor(f"out_{i}_dram", shape, dt, kind="ExternalOutput").ap())
    hybrid_block(nc, *args)
    r = _run(nc, [arrays], core_ids=[0])
    got = tuple(r.results[0][f"out_{i}_dram"] for i in range(len(_OUTS)))
    return got[0]
```
